# Optimizing a Trainium2 kernel written in Bass

```python
import math
import jax, jax.numpy as jnp
from jax import lax
import numpy as np

D_MODEL = 1024
BATCH = 1
SEQ = 256
DEPTH = 2

GRID_W = 64
CTX_LEN = 256
EPS = 1e-6
N_MOD = 6

SSD_EXPAND = 2
D_INNER = SSD_EXPAND * D_MODEL
SSD_HEAD_DIM = 64
SSD_HEADS = D_INNER // SSD_HEAD_DIM
SSD_GROUPS = 8
D_STATE = 128
CONV_K = 5
CHUNK = 128
GN = SSD_GROUPS * D_STATE
CONV_CH = D_INNER + 2 * GN
SSD_IN = D_INNER + CONV_CH + 2 * SSD_HEADS

Q_HEADS = 16
KV_HEADS = 4
Q_PER_KV = Q_HEADS // KV_HEADS
HEAD_DIM = 64
Q_W = Q_HEADS * HEAD_DIM
KV_W = KV_HEADS * HEAD_DIM
WINDOW = 128
BLOCK = 128
ROPE_BASE = 10000.0
AXIS_DIM = HEAD_DIM // 2
ROPE_FREQS = AXIS_DIM // 2

D_FF = 2816
N_EXPERTS = 8
TOP_K = 2
D_FF_EXPERT = 3584

N_SSD = (DEPTH + 1) // 2
N_ATTN = DEPTH // 2
N_DENSE = (DEPTH + 1) // 2
N_MOE = DEPTH // 2

kernel_name = 'hybrid_ssd_swa_moe_dit_block'

F32 = jnp.float32

def rmsnorm(x, w):
    xf = x.astype(F32)
    y = xf * lax.rsqrt(jnp.mean(xf * xf, axis=-1, keepdims=True) + EPS)
    return (y * w.astype(F32)).astype(x.dtype)

def modulate(h, shift, scale):
    return h * (1 + scale[:, None, :]) + shift[:, None, :]

def swiglu(h, w1, w3, w2):
    return (jax.nn.silu(h @ w1) * (h @ w3)) @ w2

def moe_swiglu(h, router, w1, w3, w2):
    shp = h.shape
    t = h.reshape(-1, shp[-1])
    logits = (t @ router).astype(F32)
    top_v, top_i = lax.top_k(logits, TOP_K)
    gates = jax.nn.softmax(top_v, axis=-1)
    combine = jnp.einsum('tk,tke->te', gates, jax.nn.one_hot(top_i, N_EXPERTS, dtype=F32)).astype(h.dtype)
    out = jnp.zeros_like(t)
    for e in range(N_EXPERTS):
        out = out + combine[:, e:e + 1] * swiglu(t, w1[e], w3[e], w2[e])
    return out.reshape(shp)

def depthwise_conv_same(x, w, b):
    pad = CONV_K // 2
    n = x.shape[1]
    xp = jnp.pad(x, ((0, 0), (pad, pad), (0, 0)))
    return sum(xp[:, k:k + n] * w[k] for k in range(CONV_K)) + b

def ssd_chunked(xs, dt, a_diag, bm, cm):
    b, t, h, p = xs.shape
    g, n = bm.shape[2], bm.shape[3]
    r = h // g
    nc = t // CHUNK

    def chunks(a):
        return jnp.moveaxis(a.astype(F32).reshape((b, nc, CHUNK) + a.shape[2:]), 1, 0)

    xc = chunks(xs.reshape(b, t, g, r, p))
    dtc = chunks(dt.reshape(b, t, g, r))
    ac = dtc * a_diag.astype(F32).reshape(g, r)
    bc = chunks(bm)
    cc = chunks(cm)
    lower = jnp.tril(jnp.ones((CHUNK, CHUNK), dtype=bool))[None, :, :, None, None]

    def step(state, inp):
        x_, dt_, a_, b_, c_ = inp
        acum = jnp.cumsum(a_, axis=1)
        seg = acum[:, :, None] - acum[:, None, :]
        decay = jnp.exp(jnp.where(lower, seg, -jnp.inf))
        cb = jnp.einsum('bign,bjgn->bijg', c_, b_)
        y_intra = jnp.einsum('bijg,bijgr,bjgr,bjgrp->bigrp', cb, decay, dt_, x_)
        y_state = jnp.einsum('bign,bgrpn->bigrp', c_, state) * jnp.exp(acum)[..., None]
        tail = jnp.exp(acum[:, -1:] - acum) * dt_
        new_state = state * jnp.exp(acum[:, -1])[..., None, None] + jnp.einsum('bjgn,bjgr,bjgrp->bgrpn', b_, tail, x_)
        return new_state, y_intra + y_state

    state0 = jnp.zeros((b, g, r, p, n), F32)
    _, y = lax.scan(step, state0, (xc, dtc, ac, bc, cc))
    return jnp.moveaxis(y, 0, 1).reshape(b, t, h, p)

def gated_rmsnorm(y, z, w):
    g = (y * jax.nn.silu(z)).astype(F32)
    shp = g.shape
    g = g.reshape(shp[:-1] + (SSD_GROUPS, D_INNER // SSD_GROUPS))
    g = g * lax.rsqrt(jnp.mean(g * g, axis=-1, keepdims=True) + EPS)
    return (g.reshape(shp) * w.astype(F32)).astype(y.dtype)

def ssd_mixer(hx, hc, w_in, conv_w, conv_b, dt_bias, a_log, d_skip, norm_w, w_out):
    bsz, n_lat, _ = hx.shape
    n_ctx = hc.shape[1]

    def project(h):
        zxbcdt = h @ w_in
        z = zxbcdt[..., :D_INNER]
        xbc = jax.nn.silu(depthwise_conv_same(zxbcdt[..., D_INNER:D_INNER + CONV_CH], conv_w, conv_b))
        dt = zxbcdt[..., D_INNER + CONV_CH:]
        return z, xbc, dt

    zc, xbcc, dtc = project(hc)
    zx, xbcx, dtx = project(hx)
    z = jnp.concatenate([zc, zx], axis=1)
    xbc = jnp.concatenate([xbcc, xbcx], axis=1)
    dt_raw = jnp.concatenate([dtc, dtx], axis=1)
    total = n_ctx + n_lat
    xs = xbc[..., :D_INNER].reshape(bsz, total, SSD_HEADS, SSD_HEAD_DIM)
    bm = xbc[..., D_INNER:D_INNER + GN].reshape(bsz, total, SSD_GROUPS, D_STATE)
    cm = xbc[..., D_INNER + GN:].reshape(bsz, total, SSD_GROUPS, D_STATE)

    def reverse_segments(t):
        return jnp.concatenate([jnp.flip(t[:, :n_ctx], axis=1), jnp.flip(t[:, n_ctx:], axis=1)], axis=1)

    def direction(d, xs_d, bm_d, cm_d, dt_raw_d):
        dt_d = jax.nn.softplus((dt_raw_d[..., d * SSD_HEADS:(d + 1) * SSD_HEADS] + dt_bias[d]).astype(F32))
        a_d = -jnp.exp(a_log[d].astype(F32))
        y_d = ssd_chunked(xs_d, dt_d, a_d, bm_d, cm_d)
        return y_d + d_skip[d].astype(F32)[:, None] * xs_d.astype(F32)

    y_fwd = direction(0, xs, bm, cm, dt_raw)
    y_bwd = reverse_segments(direction(1, reverse_segments(xs), reverse_segments(bm),
                                       reverse_segments(cm), reverse_segments(dt_raw)))
    y = (y_fwd + y_bwd).reshape(bsz, total, D_INNER).astype(hx.dtype)
    out = gated_rmsnorm(y, z, norm_w) @ w_out
    return out[:, n_ctx:], out[:, :n_ctx]

def axial_rope(x, cos, sin):
    shp = x.shape
    xr = x.astype(F32).reshape(shp[:-1] + (2, 2, ROPE_FREQS))
    bshape = (1, shp[1]) + (1,) * (len(shp) - 3) + (2, 1, ROPE_FREQS)
    c = cos.reshape(bshape)
    s = sin.reshape(bshape)
    rot = jnp.stack([-xr[..., 1, :], xr[..., 0, :]], axis=-2)
    return (xr * c + rot * s).reshape(shp).astype(x.dtype)

def sink_attention(q, ks, vs, masks, sink):
    scores = []
    for k, m in zip(ks, masks):
        s = jnp.einsum('bqgrd,bkgd->bgrqk', q, k).astype(F32)
        if m is not None:
            s = jnp.where(m, s, -jnp.inf)
        scores.append(s)
    sink_col = jnp.broadcast_to(sink.astype(F32)[None, :, :, None, None], scores[0].shape[:-1] + (1,))
    p = jax.nn.softmax(jnp.concatenate(scores + [sink_col], axis=-1), axis=-1)
    out = 0
    off = 0
    for k, v in zip(ks, vs):
        n = k.shape[1]
        out = out + jnp.einsum('bgrqk,bkgd->bqgrd', p[..., off:off + n].astype(v.dtype), v)
        off += n
    return out

def window_attention(hx, hc, w_qkv, b_qkv, sink, w_o, b_o, cos, sin, need_ctx):
    bsz, n_lat, _ = hx.shape
    n_ctx = hc.shape[1]
    n_blk = n_lat // BLOCK
    scale = 1.0 / math.sqrt(HEAD_DIM)

    def project(h):
        t = h @ w_qkv + b_qkv
        l = h.shape[1]
        q = t[..., :Q_W].reshape(bsz, l, KV_HEADS, Q_PER_KV, HEAD_DIM) * scale
        k = t[..., Q_W:Q_W + KV_W].reshape(bsz, l, KV_HEADS, HEAD_DIM)
        v = t[..., Q_W + KV_W:].reshape(bsz, l, KV_HEADS, HEAD_DIM)
        return q, k, v

    qx, kx, vx = project(hx)
    qc, kc, vc = project(hc)
    qx = axial_rope(qx, cos, sin)
    kx = axial_rope(kx, cos, sin)
    pad = ((0, 0), (BLOCK, BLOCK), (0, 0), (0, 0))
    kp = jnp.pad(kx, pad)
    vp = jnp.pad(vx, pad)
    sink_gr = sink.reshape(KV_HEADS, Q_PER_KV)

    def latent_block(n):
        start = n * BLOCK
        qb = lax.dynamic_slice_in_dim(qx, start, BLOCK, axis=1)
        kb = lax.dynamic_slice_in_dim(kp, start, 3 * BLOCK, axis=1)
        vb = lax.dynamic_slice_in_dim(vp, start, 3 * BLOCK, axis=1)
        qpos = start + jnp.arange(BLOCK)
        kpos = start - BLOCK + jnp.arange(3 * BLOCK)
        mask = ((jnp.abs(qpos[:, None] - kpos[None, :]) <= WINDOW)
                & (kpos >= 0)[None, :] & (kpos < n_lat)[None, :])
        return sink_attention(qb, (kb, kc), (vb, vc), (mask, None), sink_gr)

    o = lax.map(latent_block, jnp.arange(n_blk))
    o = jnp.moveaxis(o, 0, 1).reshape(bsz, n_lat, Q_W)
    yx = o @ w_o + b_o
    if not need_ctx:
        return yx, None
    oc = sink_attention(qc, (kc,), (vc,), (None,), sink_gr).reshape(bsz, n_ctx, Q_W)
    return yx, oc @ w_o + b_o

def setup_inputs(seed: int = 0) -> dict:
    key = jax.random.key(seed)
    ks = iter(jax.random.split(key, 40))

    def nrm(shape, scale):
        return jax.random.normal(next(ks), shape, F32) * scale

    u = jax.random.uniform(next(ks), (N_SSD, 2, SSD_HEADS), F32)
    dt0 = jnp.exp(u * (math.log(0.1) - math.log(1e-3)) + math.log(1e-3))
    dt_bias = dt0 + jnp.log(-jnp.expm1(-dt0))
    a_log = jnp.log(jax.random.uniform(next(ks), (N_SSD, 2, SSD_HEADS), F32, minval=1.0, maxval=16.0))
    return {
        'x': nrm((BATCH, SEQ, D_MODEL), 1.0),
        'c': nrm((BATCH, D_MODEL), 1.0),
        'ctx': nrm((BATCH, CTX_LEN, D_MODEL), 1.0),
        'c_ctx': nrm((D_MODEL,), 1.0),
        'w_mod': nrm((DEPTH, D_MODEL, N_MOD * D_MODEL), 0.5 * D_MODEL ** -0.5),
        'b_mod': nrm((DEPTH, N_MOD * D_MODEL), 0.02),
        'norm1_w': 1.0 + nrm((DEPTH, D_MODEL), 0.02),
        'norm2_w': 1.0 + nrm((DEPTH, D_MODEL), 0.02),
        'ssd_w_in': nrm((N_SSD, D_MODEL, SSD_IN), D_MODEL ** -0.5),
        'ssd_conv_w': nrm((N_SSD, CONV_K, CONV_CH), CONV_K ** -0.5),
        'ssd_conv_b': nrm((N_SSD, CONV_CH), 0.02),
        'ssd_dt_bias': dt_bias,
        'ssd_a_log': a_log,
        'ssd_d': 1.0 + nrm((N_SSD, 2, SSD_HEADS), 0.1),
        'ssd_norm_w': 1.0 + nrm((N_SSD, D_INNER), 0.02),
        'ssd_w_out': nrm((N_SSD, D_INNER, D_MODEL), D_INNER ** -0.5),
        'attn_w_qkv': nrm((N_ATTN, D_MODEL, Q_W + 2 * KV_W), D_MODEL ** -0.5),
        'attn_b_qkv': nrm((N_ATTN, Q_W + 2 * KV_W), 0.02),
        'attn_sink': nrm((N_ATTN, Q_HEADS), 0.5),
        'attn_w_o': nrm((N_ATTN, Q_W, D_MODEL), Q_W ** -0.5),
        'attn_b_o': nrm((N_ATTN, D_MODEL), 0.02),
        'ffn_w1': nrm((N_DENSE, D_MODEL, D_FF), D_MODEL ** -0.5),
        'ffn_w3': nrm((N_DENSE, D_MODEL, D_FF), D_MODEL ** -0.5),
        'ffn_w2': nrm((N_DENSE, D_FF, D_MODEL), D_FF ** -0.5),
        'moe_router': nrm((N_MOE, D_MODEL, N_EXPERTS), D_MODEL ** -0.5),
        'moe_w1': nrm((N_MOE, N_EXPERTS, D_MODEL, D_FF_EXPERT), D_MODEL ** -0.5),
        'moe_w3': nrm((N_MOE, N_EXPERTS, D_MODEL, D_FF_EXPERT), D_MODEL ** -0.5),
        'moe_w2': nrm((N_MOE, N_EXPERTS, D_FF_EXPERT, D_MODEL), D_FF_EXPERT ** -0.5),
        'final_norm_w': 1.0 + nrm((D_MODEL,), 0.02),
    }

def reference(x, c, ctx, c_ctx, w_mod, b_mod, norm1_w, norm2_w, ssd_w_in, ssd_conv_w, ssd_conv_b,
              ssd_dt_bias, ssd_a_log, ssd_d, ssd_norm_w, ssd_w_out, attn_w_qkv, attn_b_qkv, attn_sink,
              attn_w_o, attn_b_o, ffn_w1, ffn_w3, ffn_w2, moe_router, moe_w1, moe_w3, moe_w2, final_norm_w):
    n_lat = x.shape[1]
    rows = n_lat // GRID_W
    row_ids = jnp.repeat(jnp.arange(rows), GRID_W).astype(F32)
    col_ids = jnp.tile(jnp.arange(GRID_W), rows).astype(F32)
    inv_freq = ROPE_BASE ** (-jnp.arange(ROPE_FREQS, dtype=F32) * 2.0 / AXIS_DIM)
    ang = jnp.stack([row_ids[:, None] * inv_freq, col_ids[:, None] * inv_freq], axis=1)[:, :, None, :]
    cos = jnp.cos(ang)
    sin = jnp.sin(ang)

    cx = ctx
    for i in range(DEPTH):
        last = i == DEPTH - 1
        j = i // 2
        mod_x = (jax.nn.silu(c) @ w_mod[i] + b_mod[i]).reshape(-1, N_MOD, D_MODEL)
        mod_c = (jax.nn.silu(c_ctx[None]) @ w_mod[i] + b_mod[i]).reshape(1, N_MOD, D_MODEL)

        hx = modulate(rmsnorm(x, norm1_w[i]), mod_x[:, 0], mod_x[:, 1])
        hc = modulate(rmsnorm(cx, norm1_w[i]), mod_c[:, 0], mod_c[:, 1])
        if i % 2 == 0:
            yx, yc = ssd_mixer(hx, hc, ssd_w_in[j], ssd_conv_w[j], ssd_conv_b[j], ssd_dt_bias[j],
                               ssd_a_log[j], ssd_d[j], ssd_norm_w[j], ssd_w_out[j])
        else:
            yx, yc = window_attention(hx, hc, attn_w_qkv[j], attn_b_qkv[j], attn_sink[j], attn_w_o[j],
                                      attn_b_o[j], cos, sin, not last)
        x = x + mod_x[:, 2][:, None] * yx

        hx = modulate(rmsnorm(x, norm2_w[i]), mod_x[:, 3], mod_x[:, 4])
        if last:
            h = hx
            n_ctx = 0
        else:
            cx = cx + mod_c[:, 2][:, None] * yc
            hc = modulate(rmsnorm(cx, norm2_w[i]), mod_c[:, 3], mod_c[:, 4])
            h = jnp.concatenate([hc, hx], axis=1)
            n_ctx = cx.shape[1]
        if i % 2 == 0:
            f = swiglu(h, ffn_w1[j], ffn_w3[j], ffn_w2[j])
        else:
            f = moe_swiglu(h, moe_router[j], moe_w1[j], moe_w3[j], moe_w2[j])
        x = x + mod_x[:, 5][:, None] * f[:, n_ctx:]
        if not last:
            cx = cx + mod_c[:, 5][:, None] * f[:, :n_ctx]
    return rmsnorm(x, final_norm_w)


_drawn_inputs = setup_inputs


def setup_inputs(seed=0):
    import zlib

    import numpy as np

    out = dict(_drawn_inputs(seed))
    spreads = {}
    factors = {'norm1_w': 5.49,
     'norm2_w': 3.662,
     'ssd_conv_b': 4.933,
     'ssd_d': 65.686,
     'ssd_norm_w': 6.081,
     'attn_b_qkv': 5.245,
     'attn_sink': 8.0,
     'attn_b_o': 6.064,
     'final_norm_w': 20.519}
    for name, (base, spread) in spreads.items():
        noise = np.random.default_rng([zlib.crc32(name.encode()), seed]).standard_normal(out[name].shape)
        drawn = base * np.exp(spread * noise) if base else spread * noise
        out[name] = __import__('jax').numpy.asarray(drawn.astype(out[name].dtype))
    for name, factor in factors.items():
        out[name] = (out[name] * factor).astype(out[name].dtype)
    return out
```

```python
from contextlib import ExitStack

import numpy as np

import concourse.bass as bass
from concourse import mybir

F32 = mybir.dt.float32
I32 = mybir.dt.int32
U32 = mybir.dt.uint32
ALU = mybir.AluOpType
ACT = mybir.ActivationFunctionType
AX = mybir.AxisListType

P = 128
D = 1024
KT = D // P
NTOK = 512
NCTX = 256
NLAT = 256
EPS = 1e-6

D_INNER = 2048
GROUPS = 8
GN = 1024
CONV_K = 5
HPG = 4
HEADS = 32
HD = 64
NCH = 4
SEGP = NCTX + CONV_K - 1
Q_W = 1024
KV_W = 256
D_FF = 2816
FF_BLOCKS = D_FF // 256
FF_KT = D_FF // P
E_N = 8
D_FFE = 3584
E_BLOCKS = D_FFE // 256
SLOT = 6144

V_BMOD = 0
V_N1 = 96
V_N2 = 112
V_CB = 128
V_SN = 160
V_BO = 176
V_FIN = 184
V_C = 192
V_CC = 200
V_BQ = 208
V_BK = 216
V_CW = 224

C_ID, C_ONE, C_TF, C_TB, C_TS, C_ROT = (128 * i for i in range(6))
C_COS = 768
C_SIN = 1024
C_BAND = 1280
C_IOTA = 2304
C_IOTA8 = 2432
C_N = 2440


def shape_constants():
    c = np.zeros((P, C_N), np.float32)
    i = np.arange(P)
    c[:, C_ID:C_ID + P] = np.eye(P)
    c[:, C_ONE:C_ONE + P] = 1.0
    c[:, C_TF:C_TF + P] = i[:, None] <= i[None, :]
    c[:, C_TB:C_TB + P] = i[:, None] >= i[None, :]
    c[:, C_TS:C_TS + P] = i[:, None] < i[None, :]
    for m in range(P):
        if (m // 16) % 2 == 0:
            c[m + 16, C_ROT + m] = -1.0
        else:
            c[m - 16, C_ROT + m] = 1.0
    inv = (10000.0 ** (-np.arange(16, dtype=np.float32) * np.float32(2.0) / np.float32(32))).astype(np.float32)
    t = np.arange(NLAT)
    pos = np.stack([t // 64, t % 64]).astype(np.float32)
    ang = pos[(i % 64) // 32] * inv[i % 16][:, None]
    c[:, C_COS:C_COS + NLAT] = np.cos(ang.astype(np.float32))
    c[:, C_SIN:C_SIN + NLAT] = np.sin(ang.astype(np.float32))
    for qt in range(2):
        q = qt * P + i[:, None]
        k = np.arange(NLAT)[None, :]
        c[:, C_BAND + qt * 512 + 256:C_BAND + qt * 512 + 512] = np.where(np.abs(q - k) <= 128, 0.0, -1e30)
    c[:, C_IOTA:C_IOTA + P] = i[None, :]
    c[:, C_IOTA8:C_IOTA8 + 8] = np.arange(8)[None, :]
    return c


def backbone(nc, x, c, ctx_in, c_ctx, w_mod, b_mod, norm1_w, norm2_w, w_in, conv_w, conv_b, dt_bias, a_log,
             d_skip, ssd_norm_w, w_out, w_qkv, b_qkv, sink, w_o, b_o, w1, w3, w2, router, mw1, mw3, mw2,
             final_w, consts, out):
    es = ExitStack()
    with es:
        def sb(name, n, dt=F32):
            return es.enter_context(nc.sbuf_tensor(name, [P, n], dt))

        def sem(name):
            return es.enter_context(nc.semaphore(name))

        scr = nc.dram_tensor("acum_rows", (2 * HEADS, NTOK), F32, kind="Internal").ap()

        ring = sb("ring", 2 * SLOT)
        xT = sb("xT", KT * NTOK)[:].rearrange("p (k t) -> p k t", k=KT)
        hT = sb("hT", KT * NTOK)[:].rearrange("p (k t) -> p k t", k=KT)
        cst = sb("cst", C_N)
        col = sb("col", 384)
        csT = sb("csT", 16)[:].rearrange("p (k r) -> p k r", k=8)
        modT = sb("modT", 192)[:].rearrange("p (l m r) -> p l m r", l=2, m=48)
        alpha = sb("alpha", 64)[:].rearrange("p (n k r) -> p n k r", n=4, k=8)
        dtk = sb("dtk", 256)[:].rearrange("p (c h) -> p c h", c=NCH)
        atk = sb("atk", 256)[:].rearrange("p (c h) -> p c h", c=NCH)
        acum = sb("acum", 256)[:].rearrange("p (c h) -> p c h", c=NCH)
        dec = sb("dec", 256)[:].rearrange("p (c h) -> p c h", c=NCH)
        tail = sb("tail", 256)[:].rearrange("p (c h) -> p c h", c=NCH)
        dcol = sb("dcol", 16)
        dbc = sb("dbc", 64)
        small = sb("small", 64)
        eps = small[:, 0:1]
        one = small[:, 1:2]
        dtb = small[0:64, 2:3]
        nega = small[0:64, 3:4]
        sinkc = small[:, 16:32]
        AREA = 27680
        area = sb("area", AREA)

        class At:
            def __init__(self, start, end=AREA):
                self.n, self.end = start, end

            def take(self, n):
                self.n += n
                assert self.n <= self.end, self.n
                return area[:, self.n - n:self.n]

        slots = [ring[:, 0:SLOT], ring[:, SLOT:2 * SLOT]]
        HI = AREA - 2 * SLOT
        moe_slots = [area[:, HI:HI + SLOT], area[:, HI + SLOT:AREA], slots[0], slots[1]]

        a0 = At(8192)
        sq = a0.take(4096).rearrange("p (k t) -> p k t", k=KT)
        xtm = sq.rearrange("p k t -> p (k t)").rearrange("p (a d) -> p a d", a=4)
        rs = a0.take(512)
        vrow = a0.take(384).rearrange("p (a b) -> p a b", a=3)
        dts = [a0.take(512) for _ in range(6)]
        wdt = a0.take(512).rearrange("p (k n) -> p k n", k=KT)
        a1 = At(0)
        gT = a1.take(16 * 512).rearrange("p (k t) -> p k t", k=16)
        raw = a1.take(4 * 2 * SEGP).rearrange("p (i s t) -> p i s t", i=4, s=2)
        cx = a1.take(4 * 512).rearrange("p (i t) -> p i t", i=4)
        xtok = a1.take(1024).rearrange("p (c n) -> p c n", c=NCH)
        ysq = xtok.rearrange("p c n -> p (c n)").rearrange("p (i t) -> p i t", i=2)
        btok = a1.take(512).rearrange("p (c n) -> p c n", c=NCH)
        xdt = [a1.take(1024).rearrange("p (c n) -> p c n", c=NCH) for _ in range(2)]
        xtl = [a1.take(1024).rearrange("p (c n) -> p c n", c=NCH) for _ in range(2)]
        yb = xtl[0].rearrange("p c n -> p (c n)").rearrange("p (i t) -> p i t", i=2)
        rowb = [a1.take(2048).rearrange("p (h t) -> p h t", h=HPG) for _ in range(2)]
        seg = [a1.take(2048).rearrange("p (h t) -> p h t", h=HPG) for _ in range(2)]
        zs = a1.take(1024).rearrange("p (i t) -> p i t", i=2)
        grs = a1.take(512)
        tail1 = slots[1][:, 4096:SLOT]
        stt_ = tail1[:, 0:1536].rearrange("p (s n) -> p s n", s=6)
        cbT = tail1[:, 1536:2048]
        SLOT_OF = {(0, 1): 0, (0, 2): 1, (0, 3): 2, (1, 0): 3, (1, 3): 4, (1, 2): 5}
        a2 = At(13000)
        hid = a2.take(FF_KT * 512).rearrange("p (k t) -> p k t", k=FF_KT)
        sil = [a2.take(512) for _ in range(2)]
        a3 = At(0, 8192)
        qT = a3.take(8 * 256).rearrange("p (k t) -> p k t", k=8)
        kTt = a3.take(2 * 512).rearrange("p (k t) -> p k t", k=2)
        vtk = a3.take(4 * 256).rearrange("p (k n) -> p k n", k=4)
        vb = a3.take(256)
        rt = [a3.take(256) for _ in range(2)]
        sc = [a3.take(512) for _ in range(2)]
        pT = [a3.take(512) for _ in range(2)]
        stat = a3.take(16)
        a3b = At(13000, HI)
        oT = a3b.take(8 * 256).rearrange("p (k t) -> p k t", k=8)
        a4 = At(0, 8192)
        h2k = a4.take(2048).rearrange("p (a d) -> p a d", a=2)
        xe = [a4.take(1024).rearrange("p (k s) -> p k s", k=KT) for _ in range(2)]
        macc = a4.take(2048).rearrange("p (k t) -> p k t", k=KT)
        G = a4.take(256).rearrange("p (a s) -> p a s", a=2)
        Gg = a4.take(256).rearrange("p (a s) -> p a s", a=2)
        Pg = a4.take(256)
        logit = a4.take(16).rearrange("p (a e) -> p a e", a=2)
        mx8 = a4.take(16).rearrange("p (a e) -> p a e", a=2)
        idf = a4.take(16).rearrange("p (a e) -> p a e", a=2)
        sel = a4.take(16).rearrange("p (a e) -> p a e", a=2)
        oh1 = a4.take(16).rearrange("p (a e) -> p a e", a=2)
        oh2 = a4.take(16).rearrange("p (a e) -> p a e", a=2)
        comb = a4.take(18).rearrange("p (a e) -> p a e", a=2)
        pos = a4.take(18).rearrange("p (a e) -> p a e", a=2)
        pos2 = a4.take(18).rearrange("p (a e) -> p a e", a=2)
        gts = a4.take(16)
        rw = sb("rw", 64)[:].rearrange("p (k e) -> p k e", k=KT)
        a4b = At(13000, HI)
        msil = [a4b.take(256) for _ in range(2)]
        a5 = At(8192, 12288)
        gh = [a5.take(256) for _ in range(2)]
        hTe = [a5.take(256) for _ in range(2)]
        ye = a5.take(1024)
        otm = a5.take(2048).rearrange("p (a d) -> p a d", a=2)
        idx = sb("idx", 16, U32)[:].rearrange("p (a e) -> p a e", a=2)
        flag = sb("flag", 8, I32)

        ps = [es.enter_context(nc.psum_tensor(f"ps{i}", [P, 512], F32)) for i in range(8)]

        ident = cst[:, C_ID:C_ID + P]
        ones = cst[:, C_ONE:C_ONE + P]
        trif = cst[:, C_TF:C_TF + P]
        trib = cst[:, C_TB:C_TB + P]
        tris = cst[:, C_TS:C_TS + P]
        rot = cst[:, C_ROT:C_ROT + P]
        cosb = cst[:, C_COS:C_COS + NLAT]
        sinb = cst[:, C_SIN:C_SIN + NLAT]
        iota = cst[:, C_IOTA:C_IOTA + P]
        iota8 = cst[:, C_IOTA8:C_IOTA8 + 8]

        def vc(row, n=1):
            return col[:, row:row + n] if isinstance(row, int) else col[:, bass.ds(row, n)]

        PN_MODA = 0
        PN_G0 = 4
        PN_LOOP = 5
        PN_OUT = 20
        PN_FF = 24
        PN_FF2 = 40
        PN_W2 = 43
        PN_QKV = 47
        PN_WO = 49
        N_PANELS = 51

        S = {}
        for n in """consts_in rows_in x_in misc_in rowb_in wfull0 wfull1 zero_done
            cols_ready silu_c x_banks xres moda_ps mod_done alpha_done
            n_sq n_sum n_rs n_rinv n_mul n_h
            dt_ps dt_v dt_act dt_dve dt_tr dt_tok ac_ps ac_sb ac_exp ac_tail ac_rows ac_rows_sb scr_out
            gemm_done gemm_evac conv_step cx_ready tr_ready tok_evac xs_ready st_ready st_op seg_op seg_mask
            er_done e_done m_done ce_done y_ready ys_done yg_done ysq_done gsum_done grs_done grinv_done gT_done
            dcol_op wo_done ff_done ff_sil ff_pair_free w2_done
            qw_in0 qw_in1 q_ps q_pre q_rot q_t1 qkv_free q_out v_ps v_out
            s_ps s_sm s_mx s_nm s_exp s_den s_rd s_p s_pt s_ptc s_pv o_out at_y at_y2
            lg_ps rt_op rt_act rk_ps h2_ps h2_sb flag_done
            g_op ga_ps xe_done gx_ps pg_done mh_ps msil_done gh_done mt_ps mt_sb mo_ps ye_done sc_ps macc_op
            mfull0 mfull1 mfull2 mfull3
            fin_o fin_ps fin_sb out_done""".split():
            S[n] = sem(n)
        wfull = [S["wfull0"], S["wfull1"]]
        mfull = [S[f"mfull{i}"] for i in range(4)]

        block = es.enter_context(nc.Block())

        def kview(w, c0, n):
            if isinstance(c0, int):
                return w[:, c0:c0 + n].rearrange("(k p) n -> p k n", p=P)
            return w[:, bass.ds(c0, n)].rearrange("(k p) n -> p k n", p=P)

        @block.sync
        def _(sp):
            def load4(slot, view, w, kt):
                step = -(-kt // 4)
                at = 0
                for j in range(4):
                    n = min(step, kt - at) if j < 3 else kt - at
                    sp.dma_start(view[:, at:at + n, :], w[:, at:at + n, :]).then_inc(wfull[slot], 16)
                    at += n

            def slotv(slot, kt, n):
                return slots[slot][:, 0:kt * n].rearrange("p (k n) -> p k n", k=kt)

            def load_mod(slot, l, m0, n):
                load4(slot, slotv(slot, 8, n), kview(w_mod[l], m0, n), 8)

            def load_group(slot, g):
                v = slotv(slot, 8, 768)
                win = w_in[0]
                for c0, a, n in ((D_INNER + g * 256, 0, 256), (2 * D_INNER + g * 128, 256, 128),
                                 (2 * D_INNER + GN + g * 128, 384, 128), (g * 256, 512, 256)):
                    sp.dma_start(v[:, :, a:a + n], kview(win, c0, n)).then_inc(wfull[slot], 16)

            def load_rowb(g):
                for d in range(2):
                    src = scr[bass.ds(d * HEADS + g * HPG, HPG), :] if not isinstance(g, int) else \
                        scr[d * HEADS + g * HPG:d * HEADS + g * HPG + HPG, :]
                    sp.dma_start(rowb[d], src.unsqueeze(0).to_broadcast([P, HPG, NTOK])).then_inc(S["rowb_in"], 16)

            sp.dma_start(cst[:], consts).then_inc(S["consts_in"], 16)
            sp.wait_ge(S["zero_done"], 1)
            for arr, row in ((b_mod[0], V_BMOD), (b_mod[1], V_BMOD + 48), (norm1_w[0], V_N1), (norm1_w[1], V_N1 + 8),
                             (norm2_w[0], V_N2), (norm2_w[1], V_N2 + 8), (conv_b[0], V_CB), (ssd_norm_w[0], V_SN),
                             (b_o[0], V_BO), (final_w, V_FIN), (c[0], V_C), (c_ctx, V_CC), (b_qkv[0, Q_W:Q_W + KV_W], V_BK)):
                n = arr.shape[0] // P
                sp.dma_start(vrow[row % P:row % P + n, row // P, :],
                             arr.rearrange("(t p) -> t p", p=P)).then_inc(S["rows_in"], 16)
            for g in range(2):
                for a in range(2):
                    sp.dma_start(vrow[V_BQ % P + 4 * g:V_BQ % P + 4 * g + 4, 1, a * 64:a * 64 + 64],
                                 b_qkv[0, (8 * g + 4 * a) * 64:(8 * g + 4 * a + 4) * 64]
                                 .rearrange("(i d) -> i d", d=64)).then_inc(S["rows_in"], 16)
            sp.dma_start(vrow[96:128, 1, :], conv_w[0, 0, :].rearrange("(t p) -> t p", p=P)).then_inc(S["rows_in"], 16)
            for j in range(1, CONV_K):
                sp.dma_start(vrow[(j - 1) * 32:j * 32, 2, :],
                             conv_w[0, j, :].rearrange("(t p) -> t p", p=P)).then_inc(S["rows_in"], 16)
            load_mod(0, 0, 0, 512)
            for tt in range(4):
                src = ctx_in[0] if tt < 2 else x[0]
                sp.dma_start(xtm[:, tt, :], src[(tt % 2) * P:(tt % 2) * P + P, :]).then_inc(S["x_in"], 16)
            load_mod(1, 0, 512, 512)
            with nc.allow_non_contiguous_dma(reason="64 and 128 single elements"):
                sp.dma_start(dtb, dt_bias[0].rearrange("d (h a) -> (d h) a", a=1)).then_inc(S["misc_in"], 16)
                sp.dma_start(nega, a_log[0].rearrange("d (h a) -> (d h) a", a=1)).then_inc(S["misc_in"], 16)
            sp.dma_start(dbc[:], d_skip[0].rearrange("d h -> (d h)").unsqueeze(0).to_broadcast([P, 64])).then_inc(S["misc_in"], 16)
            sp.dma_start(sinkc, sink[0].unsqueeze(0).to_broadcast([P, 16])).then_inc(S["misc_in"], 16)
            sp.dma_start(wdt, kview(w_in[0], D_INNER + 4096, 64)).then_inc(S["misc_in"], 16)
            sp.dma_start(rw, router[0].rearrange("(k p) e -> p k e", p=P)).then_inc(S["misc_in"], 16)
            sp.wait_ge(S["moda_ps"], 1)
            load_mod(0, 0, 1024, 512)
            sp.wait_ge(S["moda_ps"], 2)
            load_mod(1, 0, 1536, 512)
            sp.wait_ge(S["moda_ps"], 3)
            load_group(0, 0)
            sp.wait_ge(S["moda_ps"], 4)
            load_mod(1, 0, 2048, 512)
            sp.wait_ge(S["scr_out"], 16)
            load_rowb(0)
            sp.wait_ge(S["gemm_done"], 6)
            load_group(0, 1)
            with sp.Fori(1, 7) as i:
                sp.wait_ge(S["moda_ps"], i + 4)
                load_mod(1, 0, 2048 + i * 512, 512)
                sp.wait_ge(S["y_ready"], 2 * i)
                load_rowb(i)
                sp.wait_ge(S["gemm_done"], 6 * i + 6)
                load_group(0, i + 1)
            sp.wait_ge(S["moda_ps"], 11)
            load_mod(1, 0, 2048 + 7 * 512, 512)
            sp.wait_ge(S["y_ready"], 14)
            load_rowb(7)
            for j, (used, count) in enumerate((("gemm_done", 48), ("moda_ps", 12), ("wo_done", 2), ("wo_done", 4))):
                p = PN_OUT + j
                sp.wait_ge(S[used], count)
                load4(p % 2, slotv(p % 2, 16, 256), kview(w_out[0], j * 256, 256), 16)

            def load_ff(slot, b):
                v = slotv(slot, 8, 512)
                for w, a in ((w1[0], 0), (w3[0], 256)):
                    for h in range(2):
                        sp.dma_start(v[:, 4 * h:4 * h + 4, a:a + 256],
                                     kview(w, b * 256, 256)[:, 4 * h:4 * h + 4, :]).then_inc(wfull[slot], 16)

            sp.wait_ge(S["wo_done"], 6)
            load_ff(0, 0)
            sp.wait_ge(S["wo_done"], 8)
            load_mod(1, 1, 0, 768)
            with sp.Fori(1, 8) as i:
                sp.wait_ge(S["ff_done"], 4 * i)
                load_ff(0, i)
                sp.wait_ge(S["moda_ps"], i + 12)
                load_mod(1, 1, i * 768, 768)
            for j, (used, count) in enumerate((("ff_done", 32), ("moda_ps", 20), ("ff_done", 36))):
                sp.wait_ge(S[used], count)
                load_ff((PN_FF2 + j) % 2, 8 + j)
            for j, (used, count) in enumerate((("ff_done", 40), ("ff_done", 44), ("w2_done", 2), ("w2_done", 4))):
                p = PN_W2 + j
                sp.wait_ge(S[used], count)
                load4(p % 2, slotv(p % 2, 22, 256), kview(w2[0], j * 256, 256), 22)
            sp.dma_start(vb, b_qkv[0, Q_W + KV_W:].unsqueeze(0).to_broadcast([P, 256])).then_inc(S["misc_in"], 16)
            for j in range(2):
                p = PN_QKV + j
                sp.wait_ge(S["w2_done"], 6 + 2 * j)
                v = slotv(p % 2, 8, 768)
                for i in range(4):
                    for a in range(2):
                        sp.dma_start(v[:, :, i * P + a * 64:i * P + a * 64 + 64],
                                     kview(w_qkv[0], (8 * j + 4 * a + i) * 64, 64)).then_inc(S[f"qw_in{j}"], 16)
                for h in range(4):
                    sp.dma_start(v[:, 2 * h:2 * h + 2, 512:768],
                                 kview(w_qkv[0], Q_W + j * 256, 256)[:, 2 * h:2 * h + 2, :]).then_inc(wfull[p % 2], 16)
            for j in range(2):
                p = PN_WO + j
                sp.wait_ge(S[("q_ps", "v_ps")[j]], (6, 4)[j])
                v = slotv(p % 2, 8, 512)
                wo = w_o[0][:, j * 512:j * 512 + 512].rearrange("(g a i d) n -> g a d i n", g=2, a=2, i=4)
                for g in range(2):
                    for a in range(2):
                        sp.dma_start(v[a * 64:a * 64 + 64, 4 * g:4 * g + 4, :], wo[g, a]).then_inc(wfull[p % 2], 16)

            def experts(ps_):
                with sp.Fori(0, 4) as pr:
                    for h in range(2):
                        e = 2 * pr + h
                        for b in range(E_BLOCKS):
                            n = E_BLOCKS * h + b
                            s = n % 4
                            sp.wait_ge(S["mo_ps"], 28 * (pr + 4 * ps_) + n + 1)
                            v = moe_slots[s][:, 0:4096].rearrange("p (k n) -> p k n", k=8)
                            w1v = mw1[0][bass.ds(e, 1)].rearrange("e (k p) n -> p (e k) n", p=P)
                            w3v = mw3[0][bass.ds(e, 1)].rearrange("e (k p) n -> p (e k) n", p=P)
                            w2v = mw2[0][bass.ds(e, 1)].rearrange("e (k p) n -> p (e k) n", p=P)
                            sp.dma_start(v[:, :, 0:256], w1v[:, :, b * 256:b * 256 + 256]).then_inc(mfull[s], 16)
                            sp.dma_start(v[:, :, 256:512], w3v[:, :, b * 256:b * 256 + 256]).then_inc(mfull[s], 16)
                            for j in range(2):
                                sp.dma_start(moe_slots[s][:, 4096 + j * 1024:5120 + j * 1024],
                                             w2v[:, 2 * b + j, :]).then_inc(mfull[s], 16)

            experts(0)
            sp.wait_ge(S["flag_done"], 1)
            over = sp.value_load(flag[0:1, 0:1], min_val=0, max_val=1)
            with sp.If(over > 0):
                experts(1)
            for tt in range(2):
                sp.wait_ge(S["fin_sb"], 2 * tt + 2)
                sp.dma_start(out[0, tt * P:tt * P + P, :], otm[:, tt, :]).then_inc(S["out_done"], 16)
            sp.wait_ge(S["out_done"], 32)

        @block.gpsimd
        def _(pl):
            pl.memset(vrow, 0.0).then_inc(S["zero_done"], 1)
            def mask(g):
                for d in range(2):
                    pl.wait_ge(S["seg_op"], 2 * g + d + 1)
                    v = seg[d].rearrange("p h (c i) -> p (h c) i", c=NCH)
                    pl.affine_select(out=v, in_=v, compare_op=ALU.is_ge, fill=-1e30, base=0,
                                     pattern=[[0, 16], [1 if d == 0 else -1, P]],
                                     channel_multiplier=-1 if d == 0 else 1).then_inc(S["seg_mask"], 1)
            for g in range(GROUPS):
                mask(g)

        @block.tensor
        def _(pe):
            mm = pe.matmul

            def full(p_slot, count):
                pe.wait_ge(wfull[p_slot], 64 * count)

            def wtile(slot, kt, n, k, c0, w=P):
                return slots[slot][:, 0:kt * n].rearrange("p (k n) -> p k n", k=kt)[:, k, c0:c0 + w]

            def norm_sum(j, ntok=NTOK, t0=0):
                for k in range(KT):
                    pe.wait_ge(S["n_sq"], 8 * j + k + 1)
                    last = mm(ps[7][:, 0:ntok], ones, sq[:, k, t0:t0 + ntok], start=k == 0, stop=k == KT - 1)
                last.then_inc(S["n_sum"], 1)

            def modulation(slot, n, bank):
                for t in range(n // P):
                    for k in range(KT):
                        last = mm(ps[bank][:, 2 * t:2 * t + 2], wtile(slot, 8, n, k, t * P), csT[:, k, :],
                                  start=k == 0, stop=k == KT - 1)
                return last

            pe.wait_ge(S["consts_in"], 16)
            pe.wait_ge(S["rows_in"], 16 * 22)
            for a in range(3):
                last = pe.transpose(ps[7][:, a * P:a * P + P], vrow[:, a, :], ident)
            last.then_inc(S["x_banks"], 1)
            pe.wait_ge(S["x_in"], 64)
            pe.wait_ge(S["cols_ready"], 1)
            for k in range(KT):
                for tt in range(4):
                    last = pe.transpose(ps[k][:, tt * P:tt * P + P], xtm[:, tt, k * P:k * P + P], ident)
                last.then_inc(S["x_banks"], 1)
            pe.wait_ge(S["silu_c"], 1)
            pe.wait_ge(S["xres"], 8)
            for j in range(4):
                full(j % 2, j // 2 + 1)
                if j:
                    pe.wait_ge(S["mod_done"], j)
                last = modulation(j % 2, 512, 5)
                last.then_inc(S["moda_ps"], 1)
            norm_sum(0)
            pe.wait_ge(S["n_h"], 8)
            pe.wait_ge(S["misc_in"], 16 * 6)
            for k in range(KT):
                last = mm(ps[2][0:64, :], wdt[:, k, :], hT[:, k, :], start=k == 0, stop=k == KT - 1)
            last.then_inc(S["dt_ps"], 1)

            def gemm_tile(g, slot, t):
                T = 6 * g + t
                if not (isinstance(T, int) and T < 2):
                    pe.wait_ge(S["gemm_evac"], T - 1)
                for k in range(KT):
                    last = mm(ps[t % 2][:], wtile(slot, 8, 768, k, t * P), hT[:, k, :], start=k == 0, stop=k == KT - 1)
                return last

            full(0, 3)
            for t in range(6):
                gemm_tile(0, 0, t).then_inc(S["gemm_done"], 1)
                if t == 1:
                    pe.wait_ge(S["dt_dve"], 1)
                    for q, src in ((0, dts[4]), (1, dts[5])):
                        for ch in range(NCH):
                            o = q * 256 + ch * 64
                            last = pe.transpose(ps[3][:, o:o + 64], src[0:64, ch * P:ch * P + P], ident[0:64, 0:64])
                    last.then_inc(S["dt_tr"], 1)
                if t == 3:
                    pe.wait_ge(S["dt_tok"], 1)
                    for tri, h0, o in ((trif, 0, 0), (trib, 32, 128)):
                        mm(ps[4][:, o:o + 128], tri, atk[:, :, h0:h0 + 32], start=True, stop=True)
                    last = mm(ps[4][:, 256:512], ones, atk, start=True, stop=True)
                    last.then_inc(S["ac_ps"], 1)
            pe.wait_ge(S["ac_sb"], 1)
            for ch in range(NCH):
                last = pe.transpose(ps[2][0:64, ch * P:ch * P + P], acum[:, ch, :], ident)
            last.then_inc(S["ac_rows"], 1)

            def group_norm(g):
                for t in range(2):
                    last = mm(ps[5][:], ones, ysq[:, t, :], start=t == 0, stop=t == 1)
                last.then_inc(S["gsum_done"], 1)

            def to_tokens(g):
                pe.wait_ge(S["cx_ready"], 4 * g + 4)
                for ch in range(NCH):
                    for t in range(2):
                        o = (ch % 2) * 256 + t * P
                        last = pe.transpose(ps[2 + ch // 2][:, o:o + P], cx[:, t, ch * P:ch * P + P], ident)
                    if ch % 2:
                        last.then_inc(S["tr_ready"], 1)
                for ch in range(NCH):
                    last = pe.transpose(ps[4][:, ch * P:ch * P + P], cx[:, 2, ch * P:ch * P + P], ident)
                last.then_inc(S["tr_ready"], 1)
                for ch in range(NCH):
                    s = slice(ch * P, ch * P + P)
                    last = mm(ps[5][:, s], cx[:, 2, s], cx[:, 3, s], start=True, stop=True)
                last.then_inc(S["tr_ready"], 1)

            def states(g):
                pe.wait_ge(S["tok_evac"], 4 * g + 3)
                pe.wait_ge(S["xs_ready"], 4 * g + 2)
                for n, (d, ch) in enumerate(((0, 0), (0, 1), (0, 2), (1, 1), (1, 0), (1, 3))):
                    last = mm(ps[2 + n // 2][:, (n % 2) * 256:(n % 2) * 256 + 256], btok[:, ch, :], xtl[d][:, ch, :],
                              start=True, stop=True)
                last.then_inc(S["st_ready"], 1)

            def outputs(g):
                pe.wait_ge(S["xs_ready"], 4 * g + 4)
                pe.wait_ge(S["st_op"], 10 * g + 10)
                pe.wait_ge(S["m_done"], 2 * g + 2)
                pe.wait_ge(S["ce_done"], 2 * g + 2)
                for t in range(2):
                    for ch in range(NCH):
                        s = slice(ch * P, ch * P + P)
                        for q in range(2):
                            h = 2 * t + q
                            o = ps[6 + t][64 * q:64 * q + 64, s]
                            c0 = h * HD
                            steps = [(xdt[d][:, ch, c0:c0 + HD], seg[d][:, h, s]) for d in range(2)]
                            steps += [(stt_[:, SLOT_OF[(d, ch)], c0:c0 + HD], rowb[d][:, h, s]) for d in range(2)
                                      if (d, ch) in SLOT_OF]
                            for n, (l, r) in enumerate(steps):
                                last = mm(o, l, r, start=n == 0, stop=n == len(steps) - 1)
                    last.then_inc(S["y_ready"], 1)

            def step(i, first=False, more=True):
                if more:
                    full(0, i + 4)
                    gemm_tile(i + 1, 0, 0).then_inc(S["gemm_done"], 1)
                    gemm_tile(i + 1, 0, 1).then_inc(S["gemm_done"], 1)
                if not first:
                    pe.wait_ge(S["ysq_done"], 2 * i)
                    pe.wait_ge(S["mod_done"], i + 4)
                    group_norm(i - 1)
                    pe.wait_ge(S["grs_done"], i)
                    pe.wait_ge(S["st_op"], 10 * i)
                to_tokens(i)
                if more:
                    gemm_tile(i + 1, 0, 2).then_inc(S["gemm_done"], 1)
                    gemm_tile(i + 1, 0, 3).then_inc(S["gemm_done"], 1)
                states(i)
                full(1, i + 3)
                pe.wait_ge(S["tok_evac"], 4 * i + 4)
                modulation(1, 512, 5).then_inc(S["moda_ps"], 1)
                if not first:
                    pe.wait_ge(S["ys_done"], 2 * i)
                outputs(i)
                if more:
                    gemm_tile(i + 1, 0, 4).then_inc(S["gemm_done"], 1)
                    gemm_tile(i + 1, 0, 5).then_inc(S["gemm_done"], 1)

            pe.wait_ge(S["ac_rows_sb"], 1)
            pe.wait_ge(S["ac_exp"], 1)
            step(0, first=True)
            with pe.Fori(1, 7) as i:
                step(i)
            step(7, more=False)
            pe.wait_ge(S["ysq_done"], 16)
            pe.wait_ge(S["mod_done"], 12)
            group_norm(7)
            pe.wait_ge(S["gT_done"], 16)
            for j in range(4):
                p = PN_OUT + j
                full(p % 2, p // 2 + 1)
                for t in range(2):
                    n = 2 * j + t
                    if n >= 2:
                        pe.wait_ge(S["xres"], 8 + n - 1)
                    for k in range(16):
                        last = mm(ps[t][:], wtile(p % 2, 16, 256, k, t * P), gT[:, k, :], start=k == 0, stop=k == 15)
                    last.then_inc(S["wo_done"], 1)
            norm_sum(1)
            pe.wait_ge(S["n_h"], 16)

            def ff_block(b, slot):
                for q in range(2):
                    pe.wait_ge(S["ff_pair_free"], 2 * b + q + 1)
                    for w in range(2):
                        for k in range(KT):
                            last = mm(ps[2 * q + w][:], wtile(slot, 8, 512, k, w * 256 + q * P), hT[:, k, :],
                                      start=k == 0, stop=k == KT - 1)
                        last.then_inc(S["ff_done"], 1)

            with pe.Fori(0, 8) as i:
                full(0, i + PN_FF // 2 + 1)
                ff_block(i, 0)
                full(1, i + PN_FF // 2 + 1)
                pe.wait_ge(S["mod_done"], i + 12)
                modulation(1, 768, 5).then_inc(S["moda_ps"], 1)
            for j in range(3):
                p = PN_FF2 + j
                full(p % 2, p // 2 + 1)
                ff_block(8 + j, p % 2)
            pe.wait_ge(S["ff_pair_free"], 2 * FF_BLOCKS + 2)
            for j in range(4):
                p = PN_W2 + j
                full(p % 2, p // 2 + 1)
                for t in range(2):
                    n = 2 * j + t
                    if n >= 2:
                        pe.wait_ge(S["xres"], 16 + n - 1)
                    for k in range(FF_KT):
                        last = mm(ps[4 + t][:], wtile(p % 2, 22, 256, k, t * P), hid[:, k, :],
                                  start=k == 0, stop=k == FF_KT - 1)
                    last.then_inc(S["w2_done"], 1)
            pe.wait_ge(S["w2_done"], 8)
            pe.sem_inc(S["mo_ps"], 2)
            norm_sum(2)
            pe.wait_ge(S["n_h"], 24)

            def proj(slot, cols_of, n, t0, ntok):
                if n >= 2:
                    pe.wait_ge(S["q_pre"], n - 1)
                for k in range(KT):
                    last = mm(ps[n % 2][:, 0:ntok], cols_of(k), hT[:, k, t0:t0 + ntok], start=k == 0, stop=k == KT - 1)
                last.then_inc(S["q_ps"], 1)

            def rotate(n, src):
                pe.wait_ge(S["q_pre"], n + 1)
                if n >= 2:
                    pe.wait_ge(S["q_t1"], n - 1)
                mm(ps[2 + n % 2][:, 0:256], rot, src, start=True, stop=True).then_inc(S["q_rot"], 1)

            def columns(slot, c0):
                return lambda k: wtile(slot, 8, 768, k, c0)

            tiles = []
            for j in range(2):
                s = (PN_QKV + j) % 2
                for i in range(4):
                    tiles.append((s, columns(s, i * P), 256, 256, qT[:, 4 * j + i, :]))
                if j == 0:
                    for t in range(2):
                        tiles.append((s, columns(s, 512 + t * P), 0, 512, kTt[:, t, 256:512]))
            for n, (s, f, t0, nt, src) in enumerate(tiles):
                if n in (0, 6):
                    full(s, (PN_QKV + n // 6) // 2 + 1)
                    pe.wait_ge(S[f"qw_in{n // 6}"], 128)
                proj(s, f, n, t0, nt)
                if n:
                    rotate(n - 1, tiles[n - 1][4])
            rotate(9, tiles[9][4])
            s = (PN_QKV + 1) % 2
            for kt in range(4):
                for k in range(KT):
                    last = mm(ps[4 + kt // 2][:, (kt % 2) * 256:(kt % 2) * 256 + 256], hT[:, k, kt * P:kt * P + P],
                              wtile(s, 8, 768, k, 512, 256), start=k == 0, stop=k == KT - 1)
                last.then_inc(S["v_ps"], 1)
            pe.wait_ge(S["q_out"], 10)
            pe.wait_ge(S["v_out"], 4)

            def unit(u):
                return u // 4, (u // 2) % 2, u % 2

            def scores(u):
                t, a, qt = unit(u)
                if u >= 2:
                    pe.wait_ge(S["s_sm"], u - 1)
                r = slice(64 * a, 64 * a + 64)
                mm(ps[u % 2][:], qT[r, t, qt * P:qt * P + P], kTt[r, t // 4, :], start=True, stop=True)\
                    .then_inc(S["s_ps"], 1)

            def turn(u):
                pe.wait_ge(S["s_p"], u + 1)
                if u >= 2:
                    pe.wait_ge(S["s_ptc"], u - 1)
                for kt in range(4):
                    last = pe.transpose(ps[2 + u % 2][:, kt * P:kt * P + P], sc[u % 2][:, kt * P:kt * P + P], ident)
                last.then_inc(S["s_pt"], 1)

            def values(u):
                t, a, qt = unit(u)
                pe.wait_ge(S["s_ptc"], u + 1)
                if t >= 2 and u % 4 == 0:
                    pe.wait_ge(S["o_out"], t - 1)
                kv = (t // 4) * 2 + a
                for kt in range(4):
                    last = mm(ps[4 + t % 2][64 * a:64 * a + 64, qt * P:qt * P + P], vtk[:, kt, kv * 64:kv * 64 + 64],
                              pT[u % 2][:, kt * P:kt * P + P], start=kt == 0, stop=kt == 3)
                last.then_inc(S["s_pv"], 1)

            for u in range(34):
                if u < 32:
                    scores(u)
                if 1 <= u < 33:
                    turn(u - 1)
                if u >= 2:
                    values(u - 2)
            pe.wait_ge(S["o_out"], 8)
            for j in range(2):
                p = PN_WO + j
                full(p % 2, p // 2 + 1)
                for t in range(4):
                    n = 4 * j + t
                    if n >= 2:
                        pe.wait_ge(S["at_y"], n - 1)
                    for k in range(KT):
                        last = mm(ps[n % 2][:, 0:256], wtile(p % 2, 8, 512, k, t * P), oT[:, k, :],
                                  start=k == 0, stop=k == KT - 1)
                    last.then_inc(S["wo_done"], 1)
            pe.wait_ge(S["wo_done"], 16)
            pe.sem_inc(S["mo_ps"], 2)
            norm_sum(3, NLAT, 256)
            pe.wait_ge(S["n_h"], 32)
            for tt in range(2):
                for k in range(KT):
                    last = mm(ps[0][:, 8 * tt:8 * tt + 8], hT[:, k, 256 + tt * P:256 + tt * P + P], rw[:, k, :],
                              start=k == 0, stop=k == KT - 1)
            last.then_inc(S["lg_ps"], 1)
            for tt in range(2):
                for hf in range(2):
                    for q in range(4):
                        k = 4 * hf + q
                        last = pe.transpose(ps[2 + 2 * tt + hf][:, q * P:q * P + P],
                                            hT[:, k, 256 + tt * P:256 + tt * P + P], ident)
                    last.then_inc(S["h2_ps"], 1)
            pe.wait_ge(S["rt_op"], 12)
            mm(ps[1][:, 0:8], tris, sel[:, 0, :], start=True, stop=True)
            mm(ps[1][:, 8:16], tris, sel[:, 1, :], start=True, stop=False)
            mm(ps[1][:, 8:16], ones, sel[:, 0, :], start=False, stop=True)
            mm(ps[1][:, 16:24], ones, sel[:, 0, :], start=True, stop=False)
            mm(ps[1][:, 16:24], ones, sel[:, 1, :], start=False, stop=True).then_inc(S["rk_ps"], 1)
            pe.wait_ge(S["h2_sb"], 4)

            def gather(E, par):
                pe.wait_ge(S["g_op"], 4 * E + 2)
                pe.wait_ge(S["macc_op"], 4 * E + 1)
                for k in range(KT):
                    for tt in range(2):
                        last = mm(ps[4 + k // 4][:, (k % 4) * P:(k % 4) * P + P], h2k[:, tt, k * P:k * P + P],
                                  G[:, tt, :], start=tt == 0, stop=tt == 1)
                last.then_inc(S["ga_ps"], 1)

            def place(E):
                pe.wait_ge(S["g_op"], 4 * E + 4)
                pe.wait_ge(S["xe_done"], 2 * E + 2)
                pe.wait_ge(S["macc_op"], 4 * E + 5)
                for tt in range(2):
                    last = pe.transpose(ps[4][:, tt * P:tt * P + P], Gg[:, tt, :], ident)
                last.then_inc(S["gx_ps"], 1)

            def hidden(NP, E, h, b):
                n = E_BLOCKS * h + b
                s = n % 4
                pe.wait_ge(mfull[s], 64 * (7 * NP + n // 4 + 1))
                if b == 0:
                    pe.wait_ge(S["xe_done"], 2 * E + 2)
                pe.wait_ge(S["gh_done"], E_BLOCKS * E + b + 1)
                w = moe_slots[s][:, 0:4096].rearrange("p (k n) -> p k n", k=8)
                for k in range(KT):
                    last = mm(ps[b % 2][:], xe[h][:, k, :], w[:, k, :], start=k == 0, stop=k == KT - 1)
                last.then_inc(S["mh_ps"], 1)

            def turn_h(E, b):
                pe.wait_ge(S["gh_done"], E_BLOCKS * E + b + 3)
                pe.wait_ge(S["mt_sb"], E_BLOCKS * E + b + 1)
                for q in range(2):
                    last = pe.transpose(ps[6 + b % 2][:, q * P:q * P + P], gh[b % 2][:, q * P:q * P + P], ident)
                last.then_inc(S["mt_ps"], 1)

            def down(NP, E, h, b):
                n = E_BLOCKS * h + b
                s = n % 4
                pe.wait_ge(S["mt_sb"], E_BLOCKS * E + b + 3)
                if b == 0:
                    pe.wait_ge(S["ye_done"], 2 * E + 2)
                for q in range(2):
                    for hf in range(2):
                        o = 4096 + q * 1024 + hf * 512
                        last = mm(ps[2 + hf][:], hTe[b % 2][:, q * P:q * P + P], moe_slots[s][:, o:o + 512],
                                  start=b == 0 and q == 0, stop=b == E_BLOCKS - 1 and q == 1)
                last.then_inc(S["mo_ps"], 1)

            def scatter(E):
                pe.wait_ge(S["ye_done"], 2 * E + 4)
                pe.wait_ge(S["pg_done"], E + 1)
                pe.wait_ge(S["xe_done"], 2 * E + 4)
                for j in range(4):
                    if j >= 2:
                        pe.wait_ge(S["macc_op"], 4 * E + j + 4)
                    for q in range(2):
                        k = 2 * j + q
                        last = mm(ps[4 + j % 2][:, q * 256:q * 256 + 256], ye[:, k * P:k * P + P], Pg,
                                  start=True, stop=True)
                    last.then_inc(S["sc_ps"], 1)

            def experts(ps_):
                with pe.Fori(0, 4) as pr:
                    for h in range(2):
                        NP = pr + 4 * ps_
                        E = 2 * NP + h
                        hidden(NP, E, h, 0)
                        for b in range(E_BLOCKS):
                            if b + 1 < E_BLOCKS:
                                hidden(NP, E, h, b + 1)
                            if b == 2:
                                place(E)
                            turn_h(E, b)
                            if b:
                                down(NP, E, h, b - 1)
                            if b == 8:
                                gather(E + 1, 1 - h)
                        down(NP, E, h, E_BLOCKS - 1)
                        scatter(E)

            gather(0, 0)
            experts(0)
            pe.wait_ge(S["flag_done"], 1)
            over = pe.value_load(flag[0:1, 0:1], min_val=0, max_val=1)
            with pe.If(over > 0):
                experts(1)
            norm_sum(4, NLAT, 256)
            for tt in range(2):
                for hf in range(2):
                    for q in range(4):
                        k = 4 * hf + q
                        pe.wait_ge(S["fin_o"], k + 1)
                        last = pe.transpose(ps[2 * tt + hf][:, q * P:q * P + P],
                                            hT[:, k, tt * P:tt * P + P], ident)
                    last.then_inc(S["fin_ps"], 1)

        @block.scalar
        def _(act):
            A = act.activation

            def norm_act(j, l, base, shift, lat=False):
                t0, nt = (256, 256) if lat else (0, 512)
                for k in range(KT):
                    act.wait_ge(S["xres"], 8 * j + k + 1)
                    A(sq[:, k, t0:t0 + nt], xT[:, k, t0:t0 + nt], ACT.Square).then_inc(S["n_sq"], 1)
                act.wait_ge(S["n_sum"], j + 1)
                A(rs[:, 0:nt], ps[7][:, 0:nt], ACT.Sqrt, bias=eps, scale=1.0 / D).then_inc(S["n_rs"], 1)
                if shift is None:
                    return
                act.wait_ge(S["alpha_done"], j + 1)
                for k in range(KT):
                    act.wait_ge(S["n_mul"], 8 * j + k + 1)
                    for r in range(2):
                        if lat and r == 0:
                            continue
                        v = hT[:, k, r * 256:r * 256 + 256]
                        last = A(v, v, ACT.Identity, bias=modT[:, l, shift * 8 + k, r:r + 1],
                                 scale=alpha[:, j, k, r:r + 1])
                    last.then_inc(S["n_h"], 1)

            act.wait_ge(S["x_banks"], 1)
            A(col[:], ps[7][:, 0:384], ACT.Copy).then_inc(S["cols_ready"], 1)
            act.wait_ge(S["cols_ready"], 1)
            A(csT[:, :, 0], vc(V_CC, 8), ACT.Silu)
            A(csT[:, :, 1], vc(V_C, 8), ACT.Silu).then_inc(S["silu_c"], 1)
            act.wait_ge(S["misc_in"], 16 * 6)
            act.wait_ge(S["dcol_op"], 1)
            act.wait_ge(S["x_banks"], 9)
            norm_act(0, 0, 0, 0)
            act.wait_ge(S["dt_v"], 1)
            A(dts[1][0:64, :], dts[0][0:64, :], ACT.Abs).then_inc(S["dt_act"], 1)
            act.wait_ge(S["dt_act"], 1)
            A(dts[1][0:64, :], dts[1][0:64, :], ACT.Exp, scale=-1.0).then_inc(S["dt_act"], 1)
            A(nega, nega, ACT.Exp).then_inc(S["dt_act"], 1)
            act.wait_ge(S["dt_v"], 2)
            A(dts[3][0:64, :], dts[2][0:64, :], ACT.Ln).then_inc(S["dt_act"], 1)

            def evac_raw(g, t):
                act.wait_ge(S["gemm_done"], 6 * g + t + 1)
                A(raw[:, t, :, 2:2 + 256], ps[t % 2][:].rearrange("p (s t) -> p s t", s=2), ACT.Copy)\
                    .then_inc(S["gemm_evac"], 1)

            def evac_z(g, t):
                act.wait_ge(S["gemm_done"], 6 * g + 5 + t)
                A(zs[:, t, :], ps[t][:], ACT.Silu).then_inc(S["gemm_evac"], 1)

            act.wait_ge(S["dcol_op"], 2)
            evac_raw(0, 0)
            evac_raw(0, 1)
            act.wait_ge(S["dt_tr"], 1)
            A(dtk, ps[3][:, 0:256], ACT.Copy)
            A(atk, ps[3][:, 256:512], ACT.Copy).then_inc(S["dt_tok"], 1)
            evac_raw(0, 2)
            evac_raw(0, 3)
            act.wait_ge(S["ac_ps"], 1)
            for d in range(2):
                last = A(acum[:, :, 32 * d:32 * d + 32], ps[4][:, 128 * d:128 * d + 128].rearrange("p (c h) -> p c h", c=NCH), ACT.Copy)
            last.then_inc(S["ac_sb"], 1)
            A(dec, ps[4][:, 256:512].rearrange("p (c h) -> p c h", c=NCH), ACT.Exp).then_inc(S["ac_exp"], 1)
            evac_z(0, 0)
            evac_z(0, 1)
            act.wait_ge(S["ac_tail"], 1)
            A(tail, tail, ACT.Exp).then_inc(S["ac_exp"], 1)
            act.wait_ge(S["ac_rows"], 1)
            A(dts[2][0:64, :], ps[2][0:64, :], ACT.Copy).then_inc(S["ac_rows_sb"], 1)
            act.wait_ge(S["ac_rows_sb"], 1)
            act.dma_start(scr, dts[2][0:64, :]).then_inc(S["scr_out"], 16)
            act.wait_ge(S["scr_out"], 16)

            def step(g, first=False, more=True):
                for t in range(4):
                    act.wait_ge(S["conv_step"], 20 * g + 17 + t)
                    A(cx[:, t, :], cx[:, t, :], ACT.Silu,
                      bias=vc(V_CB + (2 * g + t if t < 2 else 16 + 8 * (t - 2) + g))).then_inc(S["cx_ready"], 1)
                if more:
                    evac_raw(g + 1, 0)
                    evac_raw(g + 1, 1)
                if not first:
                    act.wait_ge(S["gsum_done"], g)
                    A(grs, ps[5][:], ACT.Sqrt, bias=eps, scale=1.0 / 256).then_inc(S["grs_done"], 1)
                for n in range(4):
                    act.wait_ge(S["tr_ready"], 4 * g + n + 1)
                    dst = (xtok[:, 0:2, :], xtok[:, 2:4, :], btok, cbT)[n]
                    A(dst, ps[2 + n][:], ACT.Copy).then_inc(S["tok_evac"], 1)
                for d in range(2):
                    act.wait_ge(S["seg_op"], 2 * g + d + 1)
                    A(rowb[d], rowb[d], ACT.Exp).then_inc(S["er_done"], 1)
                for d in range(2):
                    act.wait_ge(S["seg_mask"], 2 * g + d + 1)
                    A(seg[d], seg[d], ACT.Exp).then_inc(S["e_done"], 1)
                if more:
                    evac_raw(g + 1, 2)
                    evac_raw(g + 1, 3)
                for t in range(2):
                    act.wait_ge(S["yg_done"], 2 * g + t + 1)
                    A(ysq[:, t, :], yb[:, t, :], ACT.Square).then_inc(S["ysq_done"], 1)
                if more:
                    evac_z(g + 1, 0)
                    evac_z(g + 1, 1)

            step(0, first=True)
            with act.Fori(1, 7) as g:
                step(g)
            step(7, more=False)
            act.wait_ge(S["gsum_done"], 8)
            A(grs, ps[5][:], ACT.Sqrt, bias=eps, scale=1.0 / 256).then_inc(S["grs_done"], 1)
            norm_act(1, 0, 0, 3)

            with act.Fori(0, FF_BLOCKS) as b:
                for q in range(2):
                    act.wait_ge(S["ff_done"], 4 * b + 2 * q + 1)
                    act.wait_ge(S["ff_pair_free"], 2 * b + q + 1)
                    A(sil[q], ps[2 * q][:], ACT.Silu).then_inc(S["ff_sil"], 1)
            norm_act(2, 1, 0, 0)

            for n in range(10):
                act.wait_ge(S["q_ps"], n + 1)
                is_k = n in (4, 5)
                if is_k:
                    A(kTt[:, n - 4, :], ps[n % 2][:], ACT.Identity, bias=vc(V_BK + n - 4)).then_inc(S["q_pre"], 1)
                else:
                    t = n if n < 4 else n - 2
                    A(qT[:, t, :], ps[n % 2][:, 0:256], ACT.Identity, bias=vc(V_BQ + t)).then_inc(S["q_pre"], 1)

            def head_of(u):
                t, a = u // 4, (u // 2) % 2
                return 8 * (t // 4) + 4 * a + t % 4

            def exp_unit(u):
                act.wait_ge(S["s_nm"], u + 1)
                o = 8 * (u % 2)
                A(stat[:, o + 3:o + 4], sinkc[:, head_of(u):head_of(u) + 1], ACT.Exp, bias=stat[:, o + 1:o + 2])
                A(sc[u % 2], sc[u % 2], ACT.Exp, bias=stat[:, o + 1:o + 2], accum_out=stat[:, o + 2:o + 3])\
                    .then_inc(S["s_exp"], 1)

            def copy_pt(u):
                act.wait_ge(S["s_pt"], u + 1)
                if u >= 2:
                    act.wait_ge(S["s_pv"], u - 1)
                A(pT[u % 2], ps[2 + u % 2][:], ACT.Copy).then_inc(S["s_ptc"], 1)

            for u in range(33):
                if u < 32:
                    exp_unit(u)
                if u >= 1:
                    copy_pt(u - 1)
            norm_act(3, 1, 0, 3, lat=True)
            act.wait_ge(S["rt_op"], 6)
            for tt in range(2):
                last = A(gts[:, tt:tt + 1], gts[:, tt:tt + 1], ACT.Exp)
            last.then_inc(S["rt_act"], 1)
            for n in range(4):
                act.wait_ge(S["h2_ps"], n + 1)
                tt, hf = n // 2, n % 2
                A(h2k[:, tt, hf * 512:hf * 512 + 512], ps[2 + n][:], ACT.Copy).then_inc(S["h2_sb"], 1)

            def xe_copy(E, par):
                act.wait_ge(S["ga_ps"], E + 1)
                for j in range(2):
                    A(xe[par][:, 4 * j:4 * j + 4, :], ps[4 + j][:], ACT.Copy).then_inc(S["xe_done"], 1)

            def experts(ps_):
                with act.Fori(0, 4) as pr:
                    for h in range(2):
                        E = 2 * (pr + 4 * ps_) + h

                        def block_silu(b):
                            act.wait_ge(S["mh_ps"], E_BLOCKS * E + b + 1)
                            A(msil[b % 2], ps[b % 2][:, 0:256], ACT.Silu).then_inc(S["msil_done"], 1)

                        block_silu(0)
                        for b in range(E_BLOCKS):
                            if b + 1 < E_BLOCKS:
                                block_silu(b + 1)
                            if b == 2:
                                act.wait_ge(S["gx_ps"], E + 1)
                                A(Pg, ps[4][:, 0:256], ACT.Copy).then_inc(S["pg_done"], 1)
                            act.wait_ge(S["mt_ps"], E_BLOCKS * E + b + 1)
                            A(hTe[b % 2], ps[6 + b % 2][:, 0:256], ACT.Copy).then_inc(S["mt_sb"], 1)
                            if b == 8:
                                xe_copy(E + 1, 1 - h)
                        act.wait_ge(S["mo_ps"], E_BLOCKS * E + E_BLOCKS + 4)
                        act.wait_ge(S["sc_ps"], 4 * E + 4)
                        for hf in range(2):
                            A(ye[:, hf * 512:hf * 512 + 512], ps[2 + hf][:], ACT.Copy).then_inc(S["ye_done"], 1)

            act.sem_inc(S["ye_done"], 2)
            act.sem_inc(S["mt_sb"], 2)
            act.sem_inc(S["sc_ps"], 4)
            xe_copy(0, 0)
            experts(0)
            act.wait_ge(S["flag_done"], 1)
            over = act.value_load(flag[0:1, 0:1], min_val=0, max_val=1)
            with act.If(over > 0):
                experts(1)
            norm_act(4, 1, 0, None, lat=True)
            for tt in range(2):
                for hf in range(2):
                    act.wait_ge(S["fin_ps"], 2 * tt + hf + 1)
                    A(otm[:, tt, hf * 512:hf * 512 + 512], ps[2 * tt + hf][:], ACT.Copy).then_inc(S["fin_sb"], 1)

        @block.vector
        def _(dv):
            TS, TT, STT = dv.tensor_scalar, dv.tensor_tensor, dv.scalar_tensor_tensor

            def norm_dve(j, lat=False):
                t0, nt = (256, 256) if lat else (0, 512)
                dv.wait_ge(S["n_rs"], j + 1)
                dv.reciprocal(rs[:, 0:nt], rs[:, 0:nt]).then_inc(S["n_rinv"], 1)
                dv.wait_ge(S["n_rinv"], j + 1)
                for k in range(KT):
                    TT(hT[:, k, t0:t0 + nt], xT[:, k, t0:t0 + nt], rs[:, 0:nt], ALU.mult).then_inc(S["n_mul"], 1)

            def alphas(j, l, scale, wrow):
                STT(alpha[:, j], modT[:, l, scale * 8:scale * 8 + 8, :], 1.0,
                    vc(wrow, 8).unsqueeze(2).to_broadcast([P, 8, 2]), ALU.add, ALU.mult).then_inc(S["alpha_done"], 1)

            def mod_out(l, t0, nt, n):
                dv.wait_ge(S["moda_ps"], n + 1)
                dst = modT[:, l, t0:t0 + nt, :] if isinstance(t0, int) else modT[:, l, bass.ds(t0, nt), :]
                TT(dst, ps[5][:, 0:2 * nt].rearrange("p (m r) -> p m r", m=nt),
                   vc(V_BMOD + 48 * l + t0, nt).unsqueeze(2).to_broadcast([P, nt, 2]), ALU.add).then_inc(S["mod_done"], 1)

            dv.memset(eps, EPS)
            dv.memset(one, 1.0).then_inc(S["dcol_op"], 1)
            for k in range(KT):
                dv.wait_ge(S["x_banks"], k + 2)
                if k == 7:
                    dv.wait_ge(S["cols_ready"], 1)
                dv.tensor_copy(xT[:, k, :], ps[k][:]).then_inc(S["xres"], 1)
            dv.wait_ge(S["misc_in"], 16 * 6)
            for j in range(4):
                mod_out(0, 4 * j, 4, j)
            dv.wait_ge(S["mod_done"], 4)
            alphas(0, 0, 1, V_N1)
            norm_dve(0)
            dv.memset(raw[:, :, :, 0:2], 0.0)
            dv.memset(raw[:, :, :, 258:260], 0.0).then_inc(S["dcol_op"], 1)
            for q in range(2):
                r = slice(64 * q, 64 * q + 64)
                last = TT(dcol[r, :], dbc[r, q:32:2], dbc[r, 32 + q:64:2], ALU.add)
            last.then_inc(S["dcol_op"], 1)
            v, e, w, lw, dt_, a_ = (t[0:64, :] for t in dts)
            dv.wait_ge(S["dt_ps"], 1)
            TS(v, ps[2][0:64, :], dtb, None, ALU.add).then_inc(S["dt_v"], 1)
            dv.wait_ge(S["dt_act"], 3)
            TS(w, e, 1.0, None, ALU.add).then_inc(S["dt_v"], 1)
            dv.wait_ge(S["dt_v"], 2)
            dv.wait_ge(S["dt_act"], 4)
            n = 2

            def link(ins):
                nonlocal n
                n += 1
                ins.then_inc(S["dt_v"], 1)
                dv.wait_ge(S["dt_v"], n)

            link(TS(w, w, -1.0, None, ALU.add))
            link(TS(a_, w, 0.0, None, ALU.is_equal))
            link(TT(w, w, a_, ALU.add))
            link(TT(a_, a_, e, ALU.mult))
            link(dv.reciprocal(w, w))
            link(TT(lw, lw, w, ALU.mult))
            link(TT(lw, lw, e, ALU.mult))
            link(TT(lw, lw, a_, ALU.add))
            link(STT(dt_, v, 0.0, lw, ALU.max, ALU.add))
            TS(a_, dt_, nega, -1.0, ALU.mult, ALU.mult).then_inc(S["dt_dve"], 1)
            dv.wait_ge(S["ac_sb"], 1)
            dv.wait_ge(S["ac_exp"], 1)
            TT(tail, ps[4][:, 256:512].rearrange("p (c h) -> p c h", c=NCH), acum, ALU.subtract).then_inc(S["ac_tail"], 1)
            dv.wait_ge(S["ac_exp"], 2)
            TT(tail, tail, dtk, ALU.mult).then_inc(S["ac_tail"], 1)
            dv.wait_ge(S["ac_tail"], 2)

            def conv_row(g, t):
                return 2 * g + t if t < 2 else 16 + 8 * (t - 2) + g

            def finish(g):
                dv.wait_ge(S["grs_done"], g)
                dv.reciprocal(grs, grs).then_inc(S["grinv_done"], 1)
                dv.wait_ge(S["grinv_done"], g)
                for t in range(2):
                    r = 2 * (g - 1) + t
                    dst = gT[:, r, :] if isinstance(r, int) else gT[:, bass.ds(r, 1), :].rearrange("p a t -> p (a t)")
                    STT(dst, yb[:, t, :], vc(V_SN + r), grs, ALU.mult, ALU.mult).then_inc(S["gT_done"], 1)

            def per_token(v, d, g):
                a = v[:, :, bass.ds(32 * d + 4 * g, 4)] if not isinstance(g, int) else v[:, :, 32 * d + 4 * g:32 * d + 4 * g + 4]
                return a

            def step(g, first=False):
                for k in range(CONV_K):
                    for t in range(4):
                        if k == 0:
                            dv.wait_ge(S["gemm_evac"], 6 * g + t + 1)
                            if t == 0 and not first:
                                dv.wait_ge(S["ys_done"], 2 * g)
                        else:
                            dv.wait_ge(S["conv_step"], 20 * g + 4 * (k - 1) + t + 1)
                        src = raw[:, t, :, k:k + 256]
                        dst = cx[:, t, :].rearrange("p (s t) -> p s t", s=2)
                        wk = vc(V_CW + 32 * k + conv_row(g, t))
                        if k == 0:
                            ins = TS(dst, src, wk, None, ALU.mult)
                        else:
                            ins = STT(dst, src, wk, dst, ALU.mult, ALU.add)
                        ins.then_inc(S["conv_step"], 1)
                if not first:
                    finish(g)
                dv.wait_ge(S["rowb_in"], 32 * g + 32)
                for d in range(2):
                    o = seg[d].rearrange("p h (c i) -> p h c i", c=NCH)
                    i0 = rowb[d].rearrange("p h (c i) -> p h c i", c=NCH)
                    for ch in range(NCH):
                        a = per_token(acum, d, g)[:, ch, :].unsqueeze(2).to_broadcast([P, HPG, P])
                        last = TT(o[:, :, ch, :], i0[:, :, ch, :], a, ALU.subtract)
                    last.then_inc(S["seg_op"], 1)
                dv.wait_ge(S["tok_evac"], 4 * g + 2)
                if not first:
                    dv.wait_ge(S["gT_done"], 2 * g)
                for f, dst in ((tail, xtl), (dtk, xdt)):
                    for d in range(2):
                        a = per_token(f, d, g).unsqueeze(3).to_broadcast([P, NCH, HPG, HD])
                        TT(dst[d].rearrange("p c (h q) -> p c h q", h=HPG), xtok.rearrange("p c (h q) -> p c h q", h=HPG),
                           a, ALU.mult).then_inc(S["xs_ready"], 1)
                dv.wait_ge(S["st_ready"], g + 1)
                adds = {(0, 0): ps[2][:, 0:256], (0, 1): ps[2][:, 256:512], (0, 2): ps[3][:, 0:256],
                        (1, 1): ps[3][:, 256:512], (1, 0): ps[4][:, 0:256], (1, 3): ps[4][:, 256:512]}
                n = 10 * g
                dv.tensor_copy(stt_[:, 0, :], adds[(0, 0)]).then_inc(S["st_op"], 1)
                dv.tensor_copy(stt_[:, 3, :], adds[(1, 1)]).then_inc(S["st_op"], 1)
                n = n + 2
                for lvl in range(2):
                    pair = (((0, 1 + lvl), lvl, 1 + lvl), ((1, (0, 3)[lvl]), 3 + lvl, 4 + lvl))
                    for (d, ch), s0, s1 in pair:
                        dv.wait_ge(S["st_op"], n)
                        a = per_token(dec, d, g)[:, ch, :].unsqueeze(2).to_broadcast([P, HPG, HD])
                        TT(stt_[:, s1, :].rearrange("p (h q) -> p h q", h=HPG),
                           stt_[:, s0, :].rearrange("p (h q) -> p h q", h=HPG), a, ALU.mult).then_inc(S["st_op"], 1)
                    n = n + 2
                    for (d, ch), s0, s1 in pair:
                        dv.wait_ge(S["st_op"], n)
                        TT(stt_[:, s1, :], stt_[:, s1, :], adds[(d, ch)], ALU.add).then_inc(S["st_op"], 1)
                    n = n + 2
                for d in range(2):
                    dv.wait_ge(S["er_done"], 2 * g + d + 1)
                    TT(rowb[d], rowb[d], cx[:, 3, :].unsqueeze(1).to_broadcast([P, HPG, NTOK]), ALU.mult)\
                        .then_inc(S["ce_done"], 1)
                dv.wait_ge(S["tok_evac"], 4 * g + 4)
                for d in range(2):
                    dv.wait_ge(S["e_done"], 2 * g + d + 1)
                    TT(seg[d], seg[d], cbT.unsqueeze(1).to_broadcast([P, HPG, NTOK]), ALU.mult).then_inc(S["m_done"], 1)
                mod_out(0, 16 + 4 * g, 4, 4 + g)
                for t in range(2):
                    dv.wait_ge(S["y_ready"], 2 * g + t + 1)
                    dc = dcol[:, 2 * g + t:2 * g + t + 1] if isinstance(g, int) else dcol[:, bass.ds(2 * g + t, 1)]
                    STT(yb[:, t, :], cx[:, t, :], dc, ps[6 + t][:], ALU.mult, ALU.add).then_inc(S["ys_done"], 1)
                for t in range(2):
                    dv.wait_ge(S["ys_done"], 2 * g + t + 1)
                    dv.wait_ge(S["gemm_evac"], 6 * g + 5 + t)
                    TT(yb[:, t, :], yb[:, t, :], zs[:, t, :], ALU.mult).then_inc(S["yg_done"], 1)

            dv.wait_ge(S["dcol_op"], 3)
            step(0, first=True)
            with dv.Fori(1, 7) as g:
                step(g)
            step(7)
            finish(8)
            dv.wait_ge(S["mod_done"], 12)
            alphas(1, 0, 4, V_N2)

            def residual(k, bank, l, gate):
                for r in range(2):
                    v = xT[:, k, r * 256:r * 256 + 256]
                    last = STT(v, ps[bank][:, r * 256:r * 256 + 256], modT[:, l, gate * 8 + k, r:r + 1], v,
                               ALU.mult, ALU.add)
                last.then_inc(S["xres"], 1)

            for k in range(KT):
                dv.wait_ge(S["wo_done"], k + 1)
                residual(k, k % 2, 0, 2)
            dv.sem_inc(S["ff_pair_free"], 2)
            norm_dve(1)

            def ff_mul(b):
                for q in range(2):
                    dv.wait_ge(S["ff_sil"], 2 * b + q + 1)
                    dv.wait_ge(S["ff_done"], 4 * b + 2 * q + 2)
                    r = 2 * b + q
                    dst = hid[:, r, :] if isinstance(r, int) else hid[:, bass.ds(r, 1), :].rearrange("p a t -> p (a t)")
                    TT(dst, sil[q], ps[2 * q + 1][:], ALU.mult).then_inc(S["ff_pair_free"], 1)

            with dv.Fori(0, 8) as b:
                ff_mul(b)
                mod_out(1, 6 * b, 6, 12 + b)
            for b in range(8, FF_BLOCKS):
                ff_mul(b)
            dv.wait_ge(S["mod_done"], 20)
            alphas(2, 1, 1, V_N1 + 8)
            alphas(3, 1, 4, V_N2 + 8)
            for k in range(KT):
                dv.wait_ge(S["w2_done"], k + 1)
                residual(k, 4 + k % 2, 0, 5)
            norm_dve(2)

            for n in range(10):
                is_k = n in (4, 5)
                t = n - 4 if is_k else (n if n < 4 else n - 2)
                v = kTt[:, t, 256:512] if is_k else qT[:, t, :]
                dv.wait_ge(S["q_rot"], n + 1)
                if n >= 2:
                    dv.wait_ge(S["q_out"], n - 1)
                TT(rt[n % 2], ps[2 + n % 2][:, 0:256], sinb, ALU.mult).then_inc(S["q_t1"], 1)
                TT(v, v, cosb, ALU.mult).then_inc(S["qkv_free"], 1)
                dv.wait_ge(S["qkv_free"], n + 1)
                TT(v, v, rt[n % 2], ALU.add).then_inc(S["q_out"], 1)
            dv.wait_ge(S["misc_in"], 16 * 7)
            for kt in range(4):
                dv.wait_ge(S["v_ps"], kt + 1)
                if kt % 2:
                    TT(vtk[:, kt, :], ps[4 + kt // 2][:, 256:512], vb, ALU.add).then_inc(S["v_out"], 1)
                else:
                    dv.wait_ge(S["v_ps"], kt + 2)
                    TT(vtk[:, kt, :], ps[4 + kt // 2][:, 0:256], vb, ALU.add).then_inc(S["v_out"], 1)

            def head_of(u):
                t, a = u // 4, (u // 2) % 2
                return 8 * (t // 4) + 4 * a + t % 4

            def soft_a(u):
                o = 8 * (u % 2)
                dv.wait_ge(S["s_ps"], u + 1)
                if u >= 2:
                    dv.wait_ge(S["s_pt"], u - 1)
                b0 = C_BAND + 512 * (u % 2)
                STT(sc[u % 2], ps[u % 2][:], 0.125, cst[:, b0:b0 + 512], ALU.mult, ALU.add).then_inc(S["s_sm"], 1)
                dv.wait_ge(S["s_sm"], u + 1)
                dv.reduce_max(stat[:, o:o + 1], sc[u % 2], AX.X).then_inc(S["s_mx"], 1)
                dv.wait_ge(S["s_mx"], u + 1)
                TS(stat[:, o + 1:o + 2], stat[:, o:o + 1], sinkc[:, head_of(u):head_of(u) + 1], -1.0,
                   ALU.max, ALU.mult).then_inc(S["s_nm"], 1)

            def soft_b(u):
                o = 8 * (u % 2)
                dv.wait_ge(S["s_exp"], u + 1)
                TT(stat[:, o + 4:o + 5], stat[:, o + 2:o + 3], stat[:, o + 3:o + 4], ALU.add).then_inc(S["s_den"], 1)
                dv.wait_ge(S["s_den"], u + 1)
                dv.reciprocal(stat[:, o + 5:o + 6], stat[:, o + 4:o + 5]).then_inc(S["s_rd"], 1)
                dv.wait_ge(S["s_rd"], u + 1)
                TS(sc[u % 2], sc[u % 2], stat[:, o + 5:o + 6], None, ALU.mult).then_inc(S["s_p"], 1)

            for u in range(33):
                if u < 32:
                    soft_a(u)
                if u >= 1:
                    soft_b(u - 1)
                    if (u - 1) % 4 == 1 and u > 4:
                        t = (u - 1) // 4 - 1
                        dv.wait_ge(S["s_pv"], 4 * t + 4)
                        dv.tensor_copy(oT[:, t, :], ps[4 + t % 2][:, 0:256]).then_inc(S["o_out"], 1)
            dv.wait_ge(S["s_pv"], 32)
            dv.tensor_copy(oT[:, 7, :], ps[5][:, 0:256]).then_inc(S["o_out"], 1)
            for k in range(KT):
                dv.wait_ge(S["wo_done"], 8 + k + 1)
                if k >= 2:
                    dv.wait_ge(S["xres"], 24 + k - 1)
                TS(rt[k % 2], ps[k % 2][:, 0:256], vc(V_BO + k), modT[:, 1, 16 + k, 1:2], ALU.add, ALU.mult)\
                    .then_inc(S["at_y"], 1)
                dv.wait_ge(S["at_y"], k + 1)
                v = xT[:, k, 256:512]
                TT(v, v, rt[k % 2], ALU.add).then_inc(S["xres"], 1)
            norm_dve(3, lat=True)

            dv.wait_ge(S["lg_ps"], 1)
            r = 0

            def rlink(ins):
                nonlocal r
                r += 1
                ins.then_inc(S["rt_op"], 1)
                dv.wait_ge(S["rt_op"], r)

            rlink(dv.tensor_copy(logit, ps[0][:, 0:16].rearrange("p (a e) -> p a e", a=2)))
            rlink(dv.max(mx8[:, 0, :], logit[:, 0, :]))
            rlink(dv.max(mx8[:, 1, :], logit[:, 1, :]))
            dv.max_index(idx[:, 0, :], mx8[:, 0, :], logit[:, 0, :])
            rlink(dv.max_index(idx[:, 1, :], mx8[:, 1, :], logit[:, 1, :]))
            rlink(dv.tensor_copy(idf, idx))
            rlink(TT(gts[:, 0:2], mx8[:, :, 1], mx8[:, :, 0], ALU.subtract))
            for tt in range(2):
                TS(oh1[:, tt, :], iota8, idf[:, tt, 0:1], None, ALU.is_equal)
            rlink(TS(oh2[:, 0, :], iota8, idf[:, 0, 1:2], None, ALU.is_equal))
            rlink(TS(oh2[:, 1, :], iota8, idf[:, 1, 1:2], None, ALU.is_equal))
            dv.wait_ge(S["rt_act"], 1)
            rlink(TS(gts[:, 2:4], gts[:, 0:2], 1.0, None, ALU.add))
            rlink(dv.reciprocal(gts[:, 4:6], gts[:, 2:4]))
            rlink(TT(gts[:, 6:8], gts[:, 0:2], gts[:, 4:6], ALU.mult))
            rlink(TT(sel, oh1, oh2, ALU.add))
            for tt in range(2):
                TS(oh1[:, tt, :], oh1[:, tt, :], gts[:, 4 + tt:5 + tt], None, ALU.mult)
            rlink(dv.memset(macc, 0.0))
            for tt in range(2):
                rlink(STT(comb[:, tt, 0:8], oh2[:, tt, :], gts[:, 6 + tt:7 + tt], oh1[:, tt, :], ALU.mult, ALU.add))
            dv.wait_ge(S["rk_ps"], 1)
            rlink(STT(pos[:, :, 0:8], ps[1][:, 0:16].rearrange("p (a e) -> p a e", a=2), 1.0, sel, ALU.add, ALU.mult))
            rlink(TS(pos[:, :, 0:8], pos[:, :, 0:8], -1.0, None, ALU.add))
            rlink(TS(pos2[:, :, 0:8], pos[:, :, 0:8], -128.0, None, ALU.add))
            dv.memset(pos2[:, :, 8:9], -1.0)
            dv.tensor_copy(comb[:, :, 8:9], comb[:, :, 0:1])
            rlink(dv.tensor_copy(pos[:, :, 8:9], pos2[:, :, 0:1]))
            rlink(dv.reduce_max(gts[:, 8:9], ps[1][:, 16:24], AX.X))
            rlink(TS(gts[:, 9:10], gts[:, 8:9], 128.0, None, ALU.is_gt))
            dv.tensor_copy(flag[:, 0:1], gts[:, 9:10]).then_inc(S["flag_done"], 1)
            dv.sem_inc(S["macc_op"], 5)
            dv.sem_inc(S["gh_done"], 2)

            def masks(E, e, pv):
                at = slice(e, e + 1) if isinstance(e, int) else bass.ds(e, 1)
                for tt in range(2):
                    TS(G[:, tt, :], iota, pv[:, tt, at], None, ALU.is_equal).then_inc(S["g_op"], 1)
                for tt in range(2):
                    TS(Gg[:, tt, :], iota, pv[:, tt, at], comb[:, tt, at], ALU.is_equal, ALU.mult).then_inc(S["g_op"], 1)

            def experts(ps_, pv):
                with dv.Fori(0, 4) as pr:
                    for h in range(2):
                        e = 2 * pr + h
                        E = 2 * (pr + 4 * ps_) + h
                        for b in range(E_BLOCKS):
                            dv.wait_ge(S["msil_done"], E_BLOCKS * E + b + 1)
                            dv.wait_ge(S["mt_sb"], E_BLOCKS * E + b + 1)
                            TT(gh[b % 2], msil[b % 2], ps[b % 2][:, 256:512], ALU.mult).then_inc(S["gh_done"], 1)
                            if b == 6:
                                dv.wait_ge(S["gx_ps"], E + 1)
                                masks(E + 1, e + 1, pv)
                        for j in range(4):
                            dv.wait_ge(S["sc_ps"], 4 * E + j + 5)
                            v = macc[:, 2 * j:2 * j + 2, :]
                            TT(v, v, ps[4 + j % 2][:].rearrange("p (a t) -> p a t", a=2), ALU.add)\
                                .then_inc(S["macc_op"], 1)

            masks(0, 0, pos)
            experts(0, pos)
            dv.wait_ge(S["macc_op"], 5 + 32)
            over = dv.value_load(flag[0:1, 0:1], min_val=0, max_val=1)
            with dv.If(over > 0):
                experts(1, pos2)
                dv.wait_ge(S["macc_op"], 5 + 64)
            for k in range(KT):
                v = xT[:, k, 256:512]
                STT(v, macc[:, k, :], modT[:, 1, 40 + k, 1:2], v, ALU.mult, ALU.add).then_inc(S["xres"], 1)
            dv.wait_ge(S["n_rs"], 5)
            dv.reciprocal(rs[:, 0:256], rs[:, 0:256]).then_inc(S["n_rinv"], 1)
            dv.wait_ge(S["n_rinv"], 5)
            for k in range(KT):
                STT(hT[:, k, 0:256], xT[:, k, 256:512], vc(V_FIN + k), rs[:, 0:256], ALU.mult, ALU.mult)\
                    .then_inc(S["fin_o"], 1)


_INS = ['x', 'c', 'ctx', 'c_ctx', 'w_mod', 'b_mod', 'norm1_w', 'norm2_w', 'ssd_w_in', 'ssd_conv_w', 'ssd_conv_b',
        'ssd_dt_bias', 'ssd_a_log', 'ssd_d', 'ssd_norm_w', 'ssd_w_out', 'attn_w_qkv', 'attn_b_qkv', 'attn_sink',
        'attn_w_o', 'attn_b_o', 'ffn_w1', 'ffn_w3', 'ffn_w2', 'moe_router', 'moe_w1', 'moe_w3', 'moe_w2',
        'final_norm_w']


def kernel(**inputs):
    import numpy as _np
    import concourse.bacc as _bacc
    from concourse import mybir as _mybir
    from concourse.bass_utils import run_bass_kernel_spmd as _run

    nc = _bacc.Bacc("TRN2", target_bir_lowering=False, num_devices=1)
    arrays, args = {}, []
    for name in _INS:
        a = _np.ascontiguousarray(inputs[name])
        arrays[f"in_{name}"] = a
        args.append(nc.dram_tensor(f"in_{name}", a.shape, _mybir.dt.from_np(a.dtype), kind="ExternalInput").ap())
    a = shape_constants()
    arrays["in_consts"] = a
    args.append(nc.dram_tensor("in_consts", a.shape, _mybir.dt.from_np(a.dtype), kind="ExternalInput").ap())
    args.append(nc.dram_tensor("out_0", (1, NLAT, D), F32, kind="ExternalOutput").ap())
    backbone(nc, *args)
    r = _run(nc, [arrays], core_ids=[0])
    return r.results[0]["out_0"]
```

```python
from contextlib import ExitStack

import numpy as np

import concourse.bass as bass
from concourse import mybir

F32 = mybir.dt.float32
F32R = mybir.dt.float32r
I32 = mybir.dt.int32
U32 = mybir.dt.uint32
ALU = mybir.AluOpType
ACT = mybir.ActivationFunctionType
AX = mybir.AxisListType

P = 128
D = 1024
KT = D // P
NTOK = 512
NCTX = 256
NLAT = 256
EPS = 1e-6

D_INNER = 2048
GROUPS = 8
GN = 1024
CONV_K = 5
HPG = 4
HEADS = 32
HD = 64
NCH = 4
SEGP = NCTX + CONV_K - 1
Q_W = 1024
KV_W = 256
D_FF = 2816
FF_BLOCKS = D_FF // 256
FF_KT = D_FF // P
E_N = 8
D_FFE = 3584
E_BLOCKS = D_FFE // 256
SLOT = 6144
STAGES = 2 * SLOT // 2048
UNITS = 8
E_LOADS = 3 * E_BLOCKS
E_UNITS = 2 * E_LOADS


def expert_order():
    order = []
    for b in range(E_BLOCKS + 1):
        if b < E_BLOCKS:
            order += [("up", b, 0), ("up", b, 1)]
        if b >= 2:
            order.append(("down", b - 2, 0))
    order.append(("down", E_BLOCKS - 1, 0))
    return order


E_ORDER = expert_order()
E_AT = {x: n for n, x in enumerate(E_ORDER)}

V_BMOD = 0
V_N1 = 96
V_N2 = 112
V_CB = 128
V_SN = 160
V_BO = 176
V_FIN = 184
V_C = 192
V_CC = 200
V_BQ = 208
V_BK = 216
V_CW = 224

C_ID, C_ONE, C_TF, C_TB, C_TS, C_ROT = (128 * i for i in range(6))
C_COS = 768
C_SIN = 1024
C_BAND = 1280
C_IOTA = 2304
C_IOTA8 = 2432
C_N = 2440


def shape_constants():
    c = np.zeros((P, C_N), np.float32)
    i = np.arange(P)
    c[:, C_ID:C_ID + P] = np.eye(P)
    c[:, C_ONE:C_ONE + P] = 1.0
    c[:, C_TF:C_TF + P] = i[:, None] <= i[None, :]
    c[:, C_TB:C_TB + P] = i[:, None] >= i[None, :]
    c[:, C_TS:C_TS + P] = i[:, None] < i[None, :]
    for m in range(P):
        if (m // 16) % 2 == 0:
            c[m + 16, C_ROT + m] = -1.0
        else:
            c[m - 16, C_ROT + m] = 1.0
    inv = (10000.0 ** (-np.arange(16, dtype=np.float32) * np.float32(2.0) / np.float32(32))).astype(np.float32)
    t = np.arange(NLAT)
    pos = np.stack([t // 64, t % 64]).astype(np.float32)
    ang = pos[(i % 64) // 32] * inv[i % 16][:, None]
    c[:, C_COS:C_COS + NLAT] = np.cos(ang.astype(np.float32))
    c[:, C_SIN:C_SIN + NLAT] = np.sin(ang.astype(np.float32))
    for qt in range(2):
        q = qt * P + i[:, None]
        k = np.arange(NLAT)[None, :]
        c[:, C_BAND + qt * 512 + 256:C_BAND + qt * 512 + 512] = np.where(np.abs(q - k) <= 128, 0.0, -1e30)
    c[:, C_IOTA:C_IOTA + P] = i[None, :]
    c[:, C_IOTA8:C_IOTA8 + 8] = np.arange(8)[None, :]
    return c


def backbone(nc, x, c, ctx_in, c_ctx, w_mod, b_mod, norm1_w, norm2_w, w_in, conv_w, conv_b, dt_bias, a_log,
             d_skip, ssd_norm_w, w_out, w_qkv, b_qkv, sink, w_o, b_o, w1, w3, w2, router, mw1, mw3, mw2,
             final_w, consts, out):
    es = ExitStack()
    with es:
        def sb(name, n, dt=F32):
            return es.enter_context(nc.sbuf_tensor(name, [P, n], dt))

        def sem(name):
            return es.enter_context(nc.semaphore(name))

        scr = nc.dram_tensor("acum_rows", (2 * HEADS, NTOK), F32, kind="Internal").ap()

        ring = sb("ring", 2 * SLOT)
        xT = sb("xT", KT * NTOK)[:].rearrange("p (k t) -> p k t", k=KT)
        hT = sb("hT", KT * NTOK)[:].rearrange("p (k t) -> p k t", k=KT)
        cst = sb("cst", C_N)
        col = sb("col", 384)
        csT = sb("csT", 16)[:].rearrange("p (k r) -> p k r", k=8)
        modT = sb("modT", 192)[:].rearrange("p (l m r) -> p l m r", l=2, m=48)
        alpha = sb("alpha", 64)[:].rearrange("p (n k r) -> p n k r", n=4, k=8)
        dtk = sb("dtk", 256)[:].rearrange("p (c h) -> p c h", c=NCH)
        atk = sb("atk", 256)[:].rearrange("p (c h) -> p c h", c=NCH)
        acum = sb("acum", 256)[:].rearrange("p (c h) -> p c h", c=NCH)
        dec = sb("dec", 256)[:].rearrange("p (c h) -> p c h", c=NCH)
        tail = sb("tail", 256)[:].rearrange("p (c h) -> p c h", c=NCH)
        dcol = sb("dcol", 16)
        dbc = sb("dbc", 64)
        small = sb("small", 64)
        eps = small[:, 0:1]
        one = small[:, 1:2]
        dtb = small[0:64, 2:3]
        nega = small[0:64, 3:4]
        sinkc = small[:, 16:32]
        idx = sb("idx", 16, U32)[:].rearrange("p (a e) -> p a e", a=2)
        flag = sb("flag", 8, I32)
        rw = sb("rw", 64)[:].rearrange("p (k e) -> p k e", k=KT)
        AREA = 27680
        E_LOW = AREA - 2 * 1024 * UNITS - 4 * 1024 - 4 * 256
        with nc.sbuf_tensor("area", [P, AREA], F32) as area:
            pass
        sb("area_low", E_LOW)
        w_hi = sb("w_hi", 1024 * UNITS, F32R)[:].rearrange("p (u n) -> p u n", u=UNITS)
        w_lo = sb("w_lo", 1024 * UNITS, F32R)[:].rearrange("p (u n) -> p u n", u=UNITS)
        x_hi = sb("x_hi", 2048, F32R)[:].rearrange("p (a k s) -> p a k s", a=2, k=KT)
        x_lo = sb("x_lo", 2048, F32R)[:].rearrange("p (a k s) -> p a k s", a=2, k=KT)
        h_hi = sb("h_hi", 512, F32R)[:].rearrange("p (a n) -> p a n", a=2)
        h_lo = sb("h_lo", 512, F32R)[:].rearrange("p (a n) -> p a n", a=2)

        class At:
            def __init__(self, start, end=AREA):
                self.n, self.end = start, end

            def take(self, n):
                self.n += n
                assert self.n <= self.end, self.n
                return area[:, self.n - n:self.n]

        slots = [ring[:, 0:SLOT], ring[:, SLOT:2 * SLOT]]
        stages = [ring[:, 2048 * i:2048 * i + 2048] for i in range(STAGES)]

        a0 = At(8192)
        sq = a0.take(4096).rearrange("p (k t) -> p k t", k=KT)
        xtm = sq.rearrange("p k t -> p (k t)").rearrange("p (a d) -> p a d", a=4)
        rs = a0.take(512)
        vrow = a0.take(384).rearrange("p (a b) -> p a b", a=3)
        dts = [a0.take(512) for _ in range(6)]
        wdt = a0.take(512).rearrange("p (k n) -> p k n", k=KT)
        a1 = At(0)
        gT = a1.take(16 * 512).rearrange("p (k t) -> p k t", k=16)
        raw = a1.take(4 * 2 * SEGP).rearrange("p (i s t) -> p i s t", i=4, s=2)
        cx = a1.take(4 * 512).rearrange("p (i t) -> p i t", i=4)
        xtok = a1.take(1024).rearrange("p (c n) -> p c n", c=NCH)
        ysq = xtok.rearrange("p c n -> p (c n)").rearrange("p (i t) -> p i t", i=2)
        btok = a1.take(512).rearrange("p (c n) -> p c n", c=NCH)
        xdt = [a1.take(1024).rearrange("p (c n) -> p c n", c=NCH) for _ in range(2)]
        xtl = [a1.take(1024).rearrange("p (c n) -> p c n", c=NCH) for _ in range(2)]
        yb = xtl[0].rearrange("p c n -> p (c n)").rearrange("p (i t) -> p i t", i=2)
        rowb = [a1.take(2048).rearrange("p (h t) -> p h t", h=HPG) for _ in range(2)]
        seg = [a1.take(2048).rearrange("p (h t) -> p h t", h=HPG) for _ in range(2)]
        zs = a1.take(1024).rearrange("p (i t) -> p i t", i=2)
        grs = a1.take(512)
        tail1 = slots[1][:, 4096:SLOT]
        stt_ = tail1[:, 0:1536].rearrange("p (s n) -> p s n", s=6)
        cbT = tail1[:, 1536:2048]
        SLOT_OF = {(0, 1): 0, (0, 2): 1, (0, 3): 2, (1, 0): 3, (1, 3): 4, (1, 2): 5}
        a2 = At(13000)
        hid = a2.take(FF_KT * 512).rearrange("p (k t) -> p k t", k=FF_KT)
        sil = [a2.take(512) for _ in range(2)]
        a3 = At(0, 8192)
        qT = a3.take(8 * 256).rearrange("p (k t) -> p k t", k=8)
        kTt = a3.take(2 * 512).rearrange("p (k t) -> p k t", k=2)
        vtk = a3.take(4 * 256).rearrange("p (k n) -> p k n", k=4)
        vb = a3.take(256)
        rt = [a3.take(256) for _ in range(2)]
        sc = [a3.take(512) for _ in range(3)]
        pT = [a3.take(512) for _ in range(2)]
        stat = a3.take(24)
        a3b = At(13000)
        oT = a3b.take(8 * 256).rearrange("p (k t) -> p k t", k=8)
        a4 = At(0, E_LOW)
        h2k = a4.take(2048).rearrange("p (a d) -> p a d", a=2)
        macc = a4.take(2048).rearrange("p (k t) -> p k t", k=KT)
        G = a4.take(256).rearrange("p (a s) -> p a s", a=2)
        Gg = a4.take(256).rearrange("p (a s) -> p a s", a=2)
        Pg = a4.take(256)
        logit = a4.take(16).rearrange("p (a e) -> p a e", a=2)
        mx8 = a4.take(16).rearrange("p (a e) -> p a e", a=2)
        idf = a4.take(16).rearrange("p (a e) -> p a e", a=2)
        sel = a4.take(16).rearrange("p (a e) -> p a e", a=2)
        oh1 = a4.take(16).rearrange("p (a e) -> p a e", a=2)
        oh2 = a4.take(16).rearrange("p (a e) -> p a e", a=2)
        comb = a4.take(18).rearrange("p (a e) -> p a e", a=2)
        pos = a4.take(18).rearrange("p (a e) -> p a e", a=2)
        pos2 = a4.take(18).rearrange("p (a e) -> p a e", a=2)
        gts = a4.take(16)
        msil = [a4.take(256) for _ in range(2)]
        gh = [a4.take(256) for _ in range(2)]
        ye = hT[:, 0:2, :].rearrange("p a t -> p (a t)")
        a5 = At(8192, 12288)
        otm = a5.take(2048).rearrange("p (a d) -> p a d", a=2)

        ps = [es.enter_context(nc.psum_tensor(f"ps{i}", [P, 512], F32)) for i in range(8)]

        ident = cst[:, C_ID:C_ID + P]
        ones = cst[:, C_ONE:C_ONE + P]
        trif = cst[:, C_TF:C_TF + P]
        trib = cst[:, C_TB:C_TB + P]
        tris = cst[:, C_TS:C_TS + P]
        rot = cst[:, C_ROT:C_ROT + P]
        cosb = cst[:, C_COS:C_COS + NLAT]
        sinb = cst[:, C_SIN:C_SIN + NLAT]
        mrow = cst[0:2, C_BAND:C_BAND + 1024]
        iota = cst[:, C_IOTA:C_IOTA + P]
        iota8 = cst[:, C_IOTA8:C_IOTA8 + 8]

        def vc(row, n=1):
            return col[:, row:row + n] if isinstance(row, int) else col[:, bass.ds(row, n)]

        PN_MODA = 0
        PN_G0 = 4
        PN_LOOP = 5
        PN_OUT = 20
        PN_FF = 24
        PN_FF2 = 40
        PN_W2 = 43
        PN_QKV = 47
        PN_WO = 49
        N_PANELS = 51

        S = {}
        for n in """consts_in rows_in x_in misc_in rowb_in wfull0 wfull1 gx_in gbc_in gz_in zero_done
            cols_ready silu_c x_banks xres moda_ps mrow_sb modt_ps mod_done alpha_done band_in
            n_sq n_sum n_rs n_rinv n_mul n_h
            dt_ps dt_v dt_act dt_dve dt_tr dt_tok ac_ps ac_sb ac_exp ac_tail ac_rows ac_rows_sb scr_out
            gemm_done gemm_evac conv_step cx_ready tr_ready tok_evac xs_ready st_ready st_op seg_op seg_mask
            er_done e_done m_done ce_done y_ready sk_done ys_done yg_done ysq_done gsum_done grs_done grinv_done gT_done
            dcol_op wo_done ff_done ff_sil ff_pair_free w2_done
            qw_in0 qw_in1 q_ps q_pre q_rot q_t1 qkv_free q_out v_ps v_out
            s_ps s_sm s_mx s_nm s_exp s_den s_rd s_p s_pt s_ptc s_pv o_out at_y at_y2
            lg_ps rt_op rt_act rk_ps h2_ps h2_sb flag_done
            g_op ga_ps xhi_done xlo_done gx_ps pg_done msil_done gh_done mt_ps hhi_done hlo_done ye_done
            sc_ps macc_op stage_in0 stage_in1 stage_in2 stage_in3 stage_in4 stage_in5 whi_done wlo_done w_used
            fin_o fin_ps fin_sb out_done""".split():
            S[n] = sem(n)
        wfull = [S["wfull0"], S["wfull1"]]
        stage_in = [S[f"stage_in{i}"] for i in range(STAGES)]

        block = es.enter_context(nc.Block())

        def kview(w, c0, n):
            if isinstance(c0, int):
                return w[:, c0:c0 + n].rearrange("(k p) n -> p k n", p=P)
            return w[:, bass.ds(c0, n)].rearrange("(k p) n -> p k n", p=P)

        @block.sync
        def _(sp):
            def load4(slot, view, w, kt):
                step = -(-kt // 4)
                at = 0
                for j in range(4):
                    n = min(step, kt - at) if j < 3 else kt - at
                    sp.dma_start(view[:, at:at + n, :], w[:, at:at + n, :]).then_inc(wfull[slot], 16)
                    at += n

            def slotv(slot, kt, n):
                return slots[slot][:, 0:kt * n].rearrange("p (k n) -> p k n", k=kt)

            def load_mod(slot, l, m0, n):
                load4(slot, slotv(slot, 8, n), kview(w_mod[l], m0, n), 8)

            group_view = slotv(0, 8, 768)

            def load_gx(g):
                sp.dma_start(group_view[:, :, 0:256], kview(w_in[0][:, D_INNER:], g * 256, 256)).then_inc(S["gx_in"], 16)

            def load_gbc(g):
                for c0, a in ((2 * D_INNER + g * 128, 256), (2 * D_INNER + GN + g * 128, 384)):
                    sp.dma_start(group_view[:, :, a:a + 128], kview(w_in[0], c0, 128)).then_inc(S["gbc_in"], 16)

            def load_gz(g):
                for c0, a in ((g * 256 + 128, 640), (g * 256, 512)):
                    sp.dma_start(group_view[:, :, a:a + 128], kview(w_in[0], c0, 128)).then_inc(S["gz_in"], 16)

            def load_rowb(g):
                for d in range(2):
                    src = scr[bass.ds(d * HEADS + g * HPG, HPG), :] if not isinstance(g, int) else \
                        scr[d * HEADS + g * HPG:d * HEADS + g * HPG + HPG, :]
                    sp.dma_start(rowb[d], src.unsqueeze(0).to_broadcast([P, HPG, NTOK])).then_inc(S["rowb_in"], 16)

            sp.dma_start(cst[:, 0:C_BAND], consts[:, 0:C_BAND]).then_inc(S["consts_in"], 16)
            sp.dma_start(cst[:, C_IOTA:C_N], consts[:, C_IOTA:C_N]).then_inc(S["band_in"], 16)
            sp.wait_ge(S["zero_done"], 1)
            for arr, row in ((b_mod[0], V_BMOD), (b_mod[1], V_BMOD + 48), (norm1_w[0], V_N1), (norm1_w[1], V_N1 + 8),
                             (norm2_w[0], V_N2), (norm2_w[1], V_N2 + 8), (conv_b[0], V_CB), (ssd_norm_w[0], V_SN),
                             (b_o[0], V_BO), (final_w, V_FIN), (c[0], V_C), (c_ctx, V_CC), (b_qkv[0, Q_W:Q_W + KV_W], V_BK)):
                n = arr.shape[0] // P
                sp.dma_start(vrow[row % P:row % P + n, row // P, :],
                             arr.rearrange("(t p) -> t p", p=P)).then_inc(S["rows_in"], 16)
            for g in range(2):
                for a in range(2):
                    sp.dma_start(vrow[V_BQ % P + 4 * g:V_BQ % P + 4 * g + 4, 1, a * 64:a * 64 + 64],
                                 b_qkv[0, (8 * g + 4 * a) * 64:(8 * g + 4 * a + 4) * 64]
                                 .rearrange("(i d) -> i d", d=64)).then_inc(S["rows_in"], 16)
            sp.dma_start(vrow[96:128, 1, :], conv_w[0, 0, :].rearrange("(t p) -> t p", p=P)).then_inc(S["rows_in"], 16)
            for j in range(1, CONV_K):
                sp.dma_start(vrow[(j - 1) * 32:j * 32, 2, :],
                             conv_w[0, j, :].rearrange("(t p) -> t p", p=P)).then_inc(S["rows_in"], 16)
            load_mod(0, 0, 0, 512)
            for tt in range(4):
                src = ctx_in[0] if tt < 2 else x[0]
                sp.dma_start(xtm[:, tt, :], src[(tt % 2) * P:(tt % 2) * P + P, :]).then_inc(S["x_in"], 16)
            load_mod(1, 0, 512, 512)
            with nc.allow_non_contiguous_dma(reason="64 and 128 single elements"):
                sp.dma_start(dtb, dt_bias[0].rearrange("d (h a) -> (d h) a", a=1)).then_inc(S["misc_in"], 16)
                sp.dma_start(nega, a_log[0].rearrange("d (h a) -> (d h) a", a=1)).then_inc(S["misc_in"], 16)
            sp.dma_start(dbc[:], d_skip[0].rearrange("d h -> (d h)").unsqueeze(0).to_broadcast([P, 64])).then_inc(S["misc_in"], 16)
            sp.dma_start(sinkc, sink[0].unsqueeze(0).to_broadcast([P, 16])).then_inc(S["misc_in"], 16)
            sp.dma_start(wdt, kview(w_in[0], D_INNER + 4096, 64)).then_inc(S["misc_in"], 16)
            sp.dma_start(rw, router[0].rearrange("(k p) e -> p k e", p=P)).then_inc(S["misc_in"], 16)
            sp.wait_ge(S["moda_ps"], 1)
            load_mod(0, 0, 1024, 512)
            sp.wait_ge(S["moda_ps"], 2)
            load_mod(1, 0, 1536, 512)
            sp.wait_ge(S["moda_ps"], 3)
            load_gx(0)
            load_gbc(0)
            load_gz(0)
            sp.wait_ge(S["moda_ps"], 4)
            load_mod(1, 0, 2048, 512)
            sp.wait_ge(S["gemm_done"], 2)
            load_gx(1)
            sp.wait_ge(S["gemm_done"], 4)
            load_gbc(1)
            sp.wait_ge(S["gemm_done"], 6)
            load_gz(1)
            sp.wait_ge(S["scr_out"], 16)
            load_rowb(0)
            with sp.Fori(1, 7) as i:
                sp.wait_ge(S["gemm_done"], 6 * i + 2)
                load_gx(i + 1)
                sp.wait_ge(S["gemm_done"], 6 * i + 4)
                load_gbc(i + 1)
                sp.wait_ge(S["moda_ps"], i + 4)
                load_mod(1, 0, 2048 + i * 512, 512)
                sp.wait_ge(S["y_ready"], 2 * i)
                load_rowb(i)
                sp.wait_ge(S["gemm_done"], 6 * i + 6)
                load_gz(i + 1)
            sp.wait_ge(S["moda_ps"], 11)
            load_mod(1, 0, 2048 + 7 * 512, 512)
            sp.wait_ge(S["y_ready"], 14)
            load_rowb(7)
            for j, (used, count) in enumerate((("gemm_done", 48), ("moda_ps", 12), ("wo_done", 2), ("wo_done", 4))):
                p = PN_OUT + j
                sp.wait_ge(S[used], count)
                load4(p % 2, slotv(p % 2, 16, 256), kview(w_out[0], j * 256, 256), 16)

            def load_ff(slot, b):
                v = slotv(slot, 8, 512)
                for w, a in ((w1[0], 0), (w3[0], 256)):
                    for h in range(2):
                        sp.dma_start(v[:, 4 * h:4 * h + 4, a:a + 256],
                                     kview(w, b * 256, 256)[:, 4 * h:4 * h + 4, :]).then_inc(wfull[slot], 16)

            sp.wait_ge(S["wo_done"], 6)
            load_ff(0, 0)
            sp.wait_ge(S["wo_done"], 8)
            load_mod(1, 1, 0, 768)
            with sp.Fori(1, 8) as i:
                sp.wait_ge(S["ff_done"], 4 * i)
                load_ff(0, i)
                sp.wait_ge(S["moda_ps"], i + 12)
                load_mod(1, 1, i * 768, 768)
            for j, (used, count) in enumerate((("ff_done", 32), ("moda_ps", 20), ("ff_done", 36))):
                sp.wait_ge(S[used], count)
                load_ff((PN_FF2 + j) % 2, 8 + j)
            for j, (used, count) in enumerate((("ff_done", 40), ("ff_done", 44), ("w2_done", 2), ("w2_done", 4))):
                p = PN_W2 + j
                sp.wait_ge(S[used], count)
                load4(p % 2, slotv(p % 2, 22, 256), kview(w2[0], j * 256, 256), 22)
            sp.wait_ge(S["mod_done"], 20)
            sp.dma_start(cst[:, C_BAND:C_IOTA], consts[:, C_BAND:C_IOTA]).then_inc(S["band_in"], 16)
            sp.dma_start(vb, b_qkv[0, Q_W + KV_W:].unsqueeze(0).to_broadcast([P, 256])).then_inc(S["misc_in"], 16)
            for j in range(2):
                p = PN_QKV + j
                sp.wait_ge(S["w2_done"], 6 + 2 * j)
                v = slotv(p % 2, 8, 768)
                for i in range(4):
                    for a in range(2):
                        sp.dma_start(v[:, :, i * P + a * 64:i * P + a * 64 + 64],
                                     kview(w_qkv[0], (8 * j + 4 * a + i) * 64, 64)).then_inc(S[f"qw_in{j}"], 16)
                for h in range(4):
                    sp.dma_start(v[:, 2 * h:2 * h + 2, 512:768],
                                 kview(w_qkv[0], Q_W + j * 256, 256)[:, 2 * h:2 * h + 2, :]).then_inc(wfull[p % 2], 16)
            for j in range(2):
                p = PN_WO + j
                sp.wait_ge(S[("q_ps", "v_ps")[j]], (6, 4)[j])
                v = slotv(p % 2, 8, 512)
                wo = w_o[0][:, j * 512:j * 512 + 512].rearrange("(g a i d) n -> g a d i n", g=2, a=2, i=4)
                for g in range(2):
                    for a in range(2):
                        sp.dma_start(v[a * 64:a * 64 + 64, 4 * g:4 * g + 4, :], wo[g, a]).then_inc(wfull[p % 2], 16)

            def experts(ps_):
                with sp.Fori(0, 4) as pr:
                    NP = pr + 4 * ps_
                    for h in range(2):
                        e = 2 * pr + h
                        w1v = mw1[0][bass.ds(e, 1)].rearrange("e (k p) n -> p (e k) n", p=P)
                        w3v = mw3[0][bass.ds(e, 1)].rearrange("e (k p) n -> p (e k) n", p=P)
                        w2v = mw2[0][bass.ds(e, 1)].rearrange("e (k p) n -> p (e k) n", p=P)
                        for n, (kind, b, half) in enumerate(E_ORDER, E_LOADS * h):
                            sp.wait_ge(S["wlo_done"], 2 * E_UNITS * NP + 2 * n + 2)
                            s = n % STAGES
                            if kind == "up":
                                v = stages[s].rearrange("p (k n) -> p k n", k=4)
                                for w, a in ((w1v, 0), (w3v, 256)):
                                    sp.dma_start(v[:, :, a:a + 256], w[:, 4 * half:4 * half + 4, b * 256:b * 256 + 256])\
                                        .then_inc(stage_in[s], 16)
                            else:
                                for j in range(2):
                                    sp.dma_start(stages[s][:, j * 1024:j * 1024 + 1024], w2v[:, 2 * b + j, :])\
                                        .then_inc(stage_in[s], 16)

            sp.wait_ge(S["wo_done"], 16)
            experts(0)
            sp.wait_ge(S["flag_done"], 1)
            over = sp.value_load(flag[0:1, 0:1], min_val=0, max_val=1)
            with sp.If(over > 0):
                experts(1)
            for tt in range(2):
                sp.wait_ge(S["fin_sb"], 2 * tt + 2)
                sp.dma_start(out[0, tt * P:tt * P + P, :], otm[:, tt, :]).then_inc(S["out_done"], 16)
            sp.wait_ge(S["out_done"], 32)

        @block.gpsimd
        def _(pl):
            pl.memset(vrow, 0.0).then_inc(S["zero_done"], 1)
            def mask(g):
                for d in range(2):
                    pl.wait_ge(S["seg_op"], 2 * g + d + 1)
                    v = seg[d].rearrange("p h (c i) -> p (h c) i", c=NCH)
                    pl.affine_select(out=v, in_=v, compare_op=ALU.is_ge, fill=-1e30, base=0,
                                     pattern=[[0, 16], [1 if d == 0 else -1, P]],
                                     channel_multiplier=-1 if d == 0 else 1).then_inc(S["seg_mask"], 1)
            for g in range(GROUPS):
                mask(g)

        @block.tensor
        def _(pe):
            mm = pe.matmul

            def full(p_slot, count):
                pe.wait_ge(wfull[p_slot], 64 * count)

            def full_panel(p):
                full(p % 2, p // 2 + 1 - (GROUPS if p % 2 == 0 and p >= PN_OUT else 0))

            def wtile(slot, kt, n, k, c0, w=P):
                return slots[slot][:, 0:kt * n].rearrange("p (k n) -> p k n", k=kt)[:, k, c0:c0 + w]

            def norm_sum(j, ntok=NTOK, t0=0):
                for k in range(KT):
                    pe.wait_ge(S["n_sq"], 8 * j + k + 1)
                    last = mm(ps[7][:, 0:ntok], ones, sq[:, k, t0:t0 + ntok], start=k == 0, stop=k == KT - 1)
                last.then_inc(S["n_sum"], 1)

            def modulation(slot, n, banks):
                w = n // len(banks)
                for j, bank in enumerate(banks):
                    for k in range(KT):
                        last = mm(ps[bank][0:2, 0:w], csT[:, k, :], wtile(slot, 8, n, k, j * w, w),
                                  start=k == 0, stop=k == KT - 1)
                last.then_inc(S["moda_ps"], 1)

            def turn_mod(i, nt, bank, at=0):
                pe.wait_ge(S["mrow_sb"], i + 1)
                for t in range(nt):
                    last = mm(ps[bank][:, 2 * t:2 * t + 2], mrow[:, at + t * P:at + t * P + P], ident[0:2, 0:2],
                              start=True, stop=True)
                last.then_inc(S["modt_ps"], 1)

            pe.wait_ge(S["consts_in"], 16)
            pe.wait_ge(S["rows_in"], 16 * 22)
            for a in range(3):
                last = pe.transpose(ps[7][:, a * P:a * P + P], vrow[:, a, :], ident)
            last.then_inc(S["x_banks"], 1)
            pe.wait_ge(S["x_in"], 64)
            pe.wait_ge(S["cols_ready"], 1)
            for k in range(KT):
                for tt in range(4):
                    last = pe.transpose(ps[k][:, tt * P:tt * P + P], xtm[:, tt, k * P:k * P + P], ident)
                last.then_inc(S["x_banks"], 1)
            pe.wait_ge(S["silu_c"], 1)
            pe.wait_ge(S["xres"], 8)
            for j in range(4):
                full(j % 2, j // 2 + 1)
                modulation(j % 2, 512, (5 + j % 2,))
                if j >= 3:
                    pe.wait_ge(S["mod_done"], j - 2)
                if j:
                    turn_mod(j - 1, 4, 3 + (j - 1) % 2, 512 * ((j - 1) % 2))
            pe.wait_ge(S["mod_done"], 2)
            turn_mod(3, 4, 4, 512)
            norm_sum(0)
            pe.wait_ge(S["misc_in"], 16 * 6)
            for k in range(KT):
                pe.wait_ge(S["n_h"], k + 1)
                last = mm(ps[2][0:64, :], wdt[:, k, :], hT[:, k, :], start=k == 0, stop=k == KT - 1)
            last.then_inc(S["dt_ps"], 1)

            def gemm_tile(g, slot, t):
                T = 6 * g + t
                if not (isinstance(T, int) and T < 2):
                    pe.wait_ge(S["gemm_evac"], T - 1)
                if t in (0, 2, 4):
                    pe.wait_ge(S[("gx_in", "gbc_in", "gz_in")[t // 2]], (16, 32, 32)[t // 2] * (g + 1))
                for k in range(KT):
                    last = mm(ps[t % 2][:], wtile(slot, 8, 768, k, t * P), hT[:, k, :], start=k == 0, stop=k == KT - 1)
                return last

            for t in range(6):
                gemm_tile(0, 0, t).then_inc(S["gemm_done"], 1)
                if t == 1:
                    pe.wait_ge(S["dt_dve"], 1)
                    for q, src in ((0, dts[4]), (1, dts[5])):
                        for ch in range(NCH):
                            o = q * 256 + ch * 64
                            last = pe.transpose(ps[3][:, o:o + 64], src[0:64, ch * P:ch * P + P], ident[0:64, 0:64])
                    last.then_inc(S["dt_tr"], 1)
                if t == 3:
                    pe.wait_ge(S["dt_tok"], 1)
                    for tri, h0, o in ((trif, 0, 0), (trib, 32, 128)):
                        mm(ps[4][:, o:o + 128], tri, atk[:, :, h0:h0 + 32], start=True, stop=True)
                    last = mm(ps[4][:, 256:512], ones, atk, start=True, stop=True)
                    last.then_inc(S["ac_ps"], 1)
            pe.wait_ge(S["ac_sb"], 1)
            for ch in range(NCH):
                last = pe.transpose(ps[2][0:64, ch * P:ch * P + P], acum[:, ch, :], ident)
            last.then_inc(S["ac_rows"], 1)

            def group_norm(g):
                for t in range(2):
                    last = mm(ps[5][:], ones, ysq[:, t, :], start=t == 0, stop=t == 1)
                last.then_inc(S["gsum_done"], 1)

            def to_tokens(g):
                pe.wait_ge(S["cx_ready"], 4 * g + 4)
                for ch in range(NCH):
                    for t in range(2):
                        o = (ch % 2) * 256 + t * P
                        last = pe.transpose(ps[2 + ch // 2][:, o:o + P], cx[:, t, ch * P:ch * P + P], ident)
                    if ch % 2:
                        last.then_inc(S["tr_ready"], 1)
                for ch in range(NCH):
                    last = pe.transpose(ps[4][:, ch * P:ch * P + P], cx[:, 2, ch * P:ch * P + P], ident)
                last.then_inc(S["tr_ready"], 1)
                for ch in range(NCH):
                    s = slice(ch * P, ch * P + P)
                    last = mm(ps[5][:, s], cx[:, 2, s], cx[:, 3, s], start=True, stop=True)
                last.then_inc(S["tr_ready"], 1)

            def states(g):
                pe.wait_ge(S["tok_evac"], 4 * g + 3)
                pe.wait_ge(S["xs_ready"], 4 * g + 2)
                for n, (d, ch) in enumerate(((0, 0), (0, 1), (0, 2), (1, 1), (1, 0), (1, 3))):
                    last = mm(ps[2 + n // 2][:, (n % 2) * 256:(n % 2) * 256 + 256], btok[:, ch, :], xtl[d][:, ch, :],
                              start=True, stop=True)
                last.then_inc(S["st_ready"], 1)

            def outputs(g):
                pe.wait_ge(S["xs_ready"], 4 * g + 4)
                pe.wait_ge(S["st_op"], 10 * g + 10)
                pe.wait_ge(S["m_done"], 2 * g + 2)
                pe.wait_ge(S["ce_done"], 2 * g + 2)
                for t in range(2):
                    for ch in range(NCH):
                        s = slice(ch * P, ch * P + P)
                        for q in range(2):
                            h = 2 * t + q
                            o = ps[6 + t][64 * q:64 * q + 64, s]
                            c0 = h * HD
                            steps = [(xdt[d][:, ch, c0:c0 + HD], seg[d][:, h, s]) for d in range(2)]
                            steps += [(stt_[:, SLOT_OF[(d, ch)], c0:c0 + HD], rowb[d][:, h, s]) for d in range(2)
                                      if (d, ch) in SLOT_OF]
                            for n, (l, r) in enumerate(steps):
                                last = mm(o, l, r, start=n == 0, stop=n == len(steps) - 1)
                    last.then_inc(S["y_ready"], 1)

            def step(i, first=False, more=True):
                if more:
                    gemm_tile(i + 1, 0, 0).then_inc(S["gemm_done"], 1)
                    gemm_tile(i + 1, 0, 1).then_inc(S["gemm_done"], 1)
                if not first:
                    pe.wait_ge(S["ysq_done"], 2 * i)
                    pe.wait_ge(S["mod_done"], i + 4)
                    group_norm(i - 1)
                    pe.wait_ge(S["grs_done"], i)
                    pe.wait_ge(S["st_op"], 10 * i)
                to_tokens(i)
                if more:
                    gemm_tile(i + 1, 0, 2).then_inc(S["gemm_done"], 1)
                    gemm_tile(i + 1, 0, 3).then_inc(S["gemm_done"], 1)
                states(i)
                full(1, i + 3)
                pe.wait_ge(S["tok_evac"], 4 * i + 4)
                modulation(1, 512, (5,))
                if not first:
                    pe.wait_ge(S["ys_done"], 2 * i)
                outputs(i)
                if more:
                    gemm_tile(i + 1, 0, 4).then_inc(S["gemm_done"], 1)
                    gemm_tile(i + 1, 0, 5).then_inc(S["gemm_done"], 1)
                turn_mod(i + 4, 4, 5)

            pe.wait_ge(S["ac_rows_sb"], 1)
            pe.wait_ge(S["ac_exp"], 1)
            step(0, first=True)
            with pe.Fori(1, 7) as i:
                step(i)
            step(7, more=False)
            pe.wait_ge(S["ysq_done"], 16)
            pe.wait_ge(S["mod_done"], 12)
            group_norm(7)
            pe.wait_ge(S["gT_done"], 16)
            for j in range(4):
                p = PN_OUT + j
                full_panel(p)
                for t in range(2):
                    n = 2 * j + t
                    if n >= 2:
                        pe.wait_ge(S["xres"], 8 + n - 1)
                    for k in range(16):
                        last = mm(ps[t][:], wtile(p % 2, 16, 256, k, t * P), gT[:, k, :], start=k == 0, stop=k == 15)
                    last.then_inc(S["wo_done"], 1)
            norm_sum(1)

            def ff_block(b, slot):
                for q in range(2):
                    pe.wait_ge(S["ff_pair_free"], 2 * b + q + 1)
                    for w in range(2):
                        for k in range(KT):
                            if q == w == 0:
                                pe.wait_ge(S["n_h"], 8 + k + 1)
                            last = mm(ps[2 * q + w][:], wtile(slot, 8, 512, k, w * 256 + q * P), hT[:, k, :],
                                      start=k == 0, stop=k == KT - 1)
                        last.then_inc(S["ff_done"], 1)

            with pe.Fori(0, 8) as i:
                full(0, i + PN_FF // 2 + 1 - GROUPS)
                ff_block(i, 0)
                full(1, i + PN_FF // 2 + 1)
                modulation(1, 768, (5, 6))
                pe.wait_ge(S["mod_done"], i + 12)
                turn_mod(i + 12, 6, 4)
            for j in range(3):
                p = PN_FF2 + j
                full_panel(p)
                ff_block(8 + j, p % 2)
            pe.wait_ge(S["ff_pair_free"], 2 * FF_BLOCKS + 2)
            for j in range(4):
                p = PN_W2 + j
                full_panel(p)
                for t in range(2):
                    n = 2 * j + t
                    if n >= 2:
                        pe.wait_ge(S["xres"], 16 + n - 1)
                    for k in range(FF_KT):
                        last = mm(ps[4 + t][:], wtile(p % 2, 22, 256, k, t * P), hid[:, k, :],
                                  start=k == 0, stop=k == FF_KT - 1)
                    last.then_inc(S["w2_done"], 1)
            norm_sum(2)

            def proj(slot, cols_of, n, t0, ntok):
                if n >= 2:
                    pe.wait_ge(S["q_pre"], n - 1)
                for k in range(KT):
                    pe.wait_ge(S["n_h"], 16 + k + 1)
                    last = mm(ps[n % 2][:, 0:ntok], cols_of(k), hT[:, k, t0:t0 + ntok], start=k == 0, stop=k == KT - 1)
                last.then_inc(S["q_ps"], 1)

            def rotate(n, src):
                pe.wait_ge(S["q_pre"], n + 1)
                if n >= 2:
                    pe.wait_ge(S["q_t1"], n - 1)
                mm(ps[2 + n % 2][:, 0:256], rot, src, start=True, stop=True).then_inc(S["q_rot"], 1)

            def columns(slot, c0):
                return lambda k: wtile(slot, 8, 768, k, c0)

            tiles = []
            for j in range(2):
                s = (PN_QKV + j) % 2
                for i in range(4):
                    tiles.append((s, columns(s, i * P), 256, 256, qT[:, 4 * j + i, :]))
                if j == 0:
                    for t in range(2):
                        tiles.append((s, columns(s, 512 + t * P), 0, 512, kTt[:, t, 256:512]))
            for n, (s, f, t0, nt, src) in enumerate(tiles):
                if n in (0, 6):
                    full_panel(PN_QKV + n // 6)
                    pe.wait_ge(S[f"qw_in{n // 6}"], 128)
                proj(s, f, n, t0, nt)
                if n:
                    rotate(n - 1, tiles[n - 1][4])
            rotate(9, tiles[9][4])
            s = (PN_QKV + 1) % 2
            for kt in range(4):
                for k in range(KT):
                    last = mm(ps[4 + kt // 2][:, (kt % 2) * 256:(kt % 2) * 256 + 256], hT[:, k, kt * P:kt * P + P],
                              wtile(s, 8, 768, k, 512, 256), start=k == 0, stop=k == KT - 1)
                last.then_inc(S["v_ps"], 1)
            pe.wait_ge(S["q_out"], 10)
            pe.wait_ge(S["v_out"], 4)

            def unit(u):
                return u // 4, (u // 2) % 2, u % 2

            def scores(u):
                t, a, qt = unit(u)
                if u >= 3:
                    pe.wait_ge(S["s_sm"], u - 2)
                r = slice(64 * a, 64 * a + 64)
                mm(ps[(0, 1, 6)[u % 3]][:], qT[r, t, qt * P:qt * P + P], kTt[r, t // 4, :], start=True, stop=True)\
                    .then_inc(S["s_ps"], 1)

            def turn(u):
                pe.wait_ge(S["s_p"], u + 1)
                if u >= 2:
                    pe.wait_ge(S["s_ptc"], u - 1)
                for kt in range(4):
                    last = pe.transpose(ps[2 + u % 2][:, kt * P:kt * P + P], sc[u % 3][:, kt * P:kt * P + P], ident)
                last.then_inc(S["s_pt"], 1)

            def values(u):
                t, a, qt = unit(u)
                pe.wait_ge(S["s_ptc"], u + 1)
                if t >= 2 and u % 4 == 0:
                    pe.wait_ge(S["o_out"], t - 1)
                kv = (t // 4) * 2 + a
                for kt in range(4):
                    last = mm(ps[4 + t % 2][64 * a:64 * a + 64, qt * P:qt * P + P], vtk[:, kt, kv * 64:kv * 64 + 64],
                              pT[u % 2][:, kt * P:kt * P + P], start=kt == 0, stop=kt == 3)
                last.then_inc(S["s_pv"], 1)

            for u in range(35):
                if u < 32:
                    scores(u)
                if 2 <= u < 34:
                    turn(u - 2)
                if u >= 3:
                    values(u - 3)
            pe.wait_ge(S["o_out"], 8)
            for j in range(2):
                p = PN_WO + j
                full_panel(p)
                for t in range(4):
                    n = 4 * j + t
                    if n >= 2:
                        pe.wait_ge(S["at_y"], n - 1)
                    for k in range(KT):
                        last = mm(ps[n % 2][:, 0:256], wtile(p % 2, 8, 512, k, t * P), oT[:, k, :],
                                  start=k == 0, stop=k == KT - 1)
                    last.then_inc(S["wo_done"], 1)
            norm_sum(3, NLAT, 256)
            pe.wait_ge(S["n_h"], 32)
            for tt in range(2):
                for k in range(KT):
                    last = mm(ps[0][:, 8 * tt:8 * tt + 8], hT[:, k, 256 + tt * P:256 + tt * P + P], rw[:, k, :],
                              start=k == 0, stop=k == KT - 1)
            last.then_inc(S["lg_ps"], 1)
            for tt in range(2):
                for hf in range(2):
                    for q in range(4):
                        k = 4 * hf + q
                        last = pe.transpose(ps[2 + 2 * tt + hf][:, q * P:q * P + P],
                                            hT[:, k, 256 + tt * P:256 + tt * P + P], ident)
                    last.then_inc(S["h2_ps"], 1)
            pe.wait_ge(S["rt_op"], 12)
            mm(ps[1][:, 0:8], tris, sel[:, 0, :], start=True, stop=True)
            mm(ps[1][:, 8:16], tris, sel[:, 1, :], start=True, stop=False)
            mm(ps[1][:, 8:16], ones, sel[:, 0, :], start=False, stop=True)
            mm(ps[1][:, 16:24], ones, sel[:, 0, :], start=True, stop=False)
            mm(ps[1][:, 16:24], ones, sel[:, 1, :], start=False, stop=True).then_inc(S["rk_ps"], 1)
            pe.wait_ge(S["h2_sb"], 4)

            def gather(E, par):
                pe.wait_ge(S["g_op"], 4 * E + 2)
                pe.wait_ge(S["macc_op"], 4 * E + 1)
                for k in range(KT):
                    for tt in range(2):
                        last = mm(ps[4 + k // 4][:, (k % 4) * P:(k % 4) * P + P], h2k[:, tt, k * P:k * P + P],
                                  G[:, tt, :], start=tt == 0, stop=tt == 1)
                last.then_inc(S["ga_ps"], 1)

            def place(E):
                pe.wait_ge(S["g_op"], 4 * E + 4)
                pe.wait_ge(S["xlo_done"], 2 * E + 2)
                pe.wait_ge(S["macc_op"], 4 * E + 5)
                for tt in range(2):
                    last = pe.transpose(ps[4][:, tt * P:tt * P + P], Gg[:, tt, :], ident)
                last.then_inc(S["gx_ps"], 1)

            def split_mm(o, hi, lo, u, c0, n, first, last):
                mm(o, hi, w_hi[:, u, c0:c0 + n], start=first, stop=False)
                mm(o, hi, w_lo[:, u, c0:c0 + n], start=False, stop=False)
                return mm(o, lo, w_hi[:, u, c0:c0 + n], start=False, stop=last)

            def hidden(NP, E, h, b):
                if b == 0:
                    pe.wait_ge(S["xlo_done"], 2 * E + 2)
                pe.wait_ge(S["gh_done"], E_BLOCKS * E + b + 1)
                for n in range(4):
                    at = E_UNITS * h + 2 * E_AT[("up", b, n // 2)] + n % 2
                    u = at % UNITS
                    pe.wait_ge(S["wlo_done"], 2 * E_UNITS * NP + at + 1 + 2 * STAGES)
                    for q in range(2):
                        k = 2 * n + q
                        last = split_mm(ps[b % 2][:], x_hi[:, h, k, :], x_lo[:, h, k, :], u, q * 512, 512, k == 0, k == KT - 1)
                    last.then_inc(S["w_used"], 1)

            def turn_h(E, b):
                pe.wait_ge(S["gh_done"], E_BLOCKS * E + b + 3)
                pe.wait_ge(S["hlo_done"], E_BLOCKS * E + b + 1)
                for q in range(2):
                    last = pe.transpose(ps[6 + b % 2][:, q * P:q * P + P], gh[b % 2][:, q * P:q * P + P], ident)
                last.then_inc(S["mt_ps"], 1)

            def down(NP, E, h, b):
                pe.wait_ge(S["hlo_done"], E_BLOCKS * E + b + 3)
                if b == 0:
                    pe.wait_ge(S["ye_done"], 2 * E + 2)
                for q in range(2):
                    at = E_UNITS * h + 2 * E_AT[("down", b, 0)] + q
                    u = at % UNITS
                    pe.wait_ge(S["wlo_done"], 2 * E_UNITS * NP + at + 1 + 2 * STAGES)
                    for hf in range(2):
                        last = split_mm(ps[2 + hf][:], h_hi[:, b % 2, q * P:q * P + P], h_lo[:, b % 2, q * P:q * P + P],
                                        u, hf * 512, 512, b == 0 and q == 0, b == E_BLOCKS - 1 and q == 1)
                    last.then_inc(S["w_used"], 1)

            def scatter(E):
                pe.wait_ge(S["ye_done"], 2 * E + 4)
                pe.wait_ge(S["pg_done"], E + 1)
                pe.wait_ge(S["xlo_done"], 2 * E + 4)
                for j in range(4):
                    if j >= 2:
                        pe.wait_ge(S["macc_op"], 4 * E + j + 4)
                    for q in range(2):
                        k = 2 * j + q
                        last = mm(ps[4 + j % 2][:, q * 256:q * 256 + 256], ye[:, k * P:k * P + P], Pg,
                                  start=True, stop=True)
                    last.then_inc(S["sc_ps"], 1)

            def experts(ps_):
                with pe.Fori(0, 4) as pr:
                    for h in range(2):
                        NP = pr + 4 * ps_
                        E = 2 * NP + h
                        hidden(NP, E, h, 0)
                        for b in range(E_BLOCKS):
                            if b + 1 < E_BLOCKS:
                                hidden(NP, E, h, b + 1)
                            if b == 2:
                                place(E)
                            turn_h(E, b)
                            if b:
                                down(NP, E, h, b - 1)
                            if b == 8:
                                gather(E + 1, 1 - h)
                        down(NP, E, h, E_BLOCKS - 1)
                        scatter(E)

            gather(0, 0)
            experts(0)
            pe.wait_ge(S["flag_done"], 1)
            over = pe.value_load(flag[0:1, 0:1], min_val=0, max_val=1)
            with pe.If(over > 0):
                experts(1)
            norm_sum(4, NLAT, 256)
            for tt in range(2):
                for hf in range(2):
                    for q in range(4):
                        k = 4 * hf + q
                        pe.wait_ge(S["fin_o"], k + 1)
                        last = pe.transpose(ps[2 * tt + hf][:, q * P:q * P + P],
                                            hT[:, k, tt * P:tt * P + P], ident)
                    last.then_inc(S["fin_ps"], 1)

        @block.scalar
        def _(act):
            A = act.activation

            def norm_act(j, l, base, shift, lat=False):
                t0, nt = (256, 256) if lat else (0, 512)
                for k in range(KT):
                    act.wait_ge(S["xres"], 8 * j + k + 1)
                    A(sq[:, k, t0:t0 + nt], xT[:, k, t0:t0 + nt], ACT.Square).then_inc(S["n_sq"], 1)
                act.wait_ge(S["n_sum"], j + 1)
                A(rs[:, 0:nt], ps[7][:, 0:nt], ACT.Sqrt, bias=eps, scale=1.0 / D).then_inc(S["n_rs"], 1)
                if shift is None:
                    return
                act.wait_ge(S["alpha_done"], j + 1)
                for k in range(KT):
                    act.wait_ge(S["n_mul"], 8 * j + k + 1)
                    for r in range(2):
                        if lat and r == 0:
                            continue
                        v = hT[:, k, r * 256:r * 256 + 256]
                        last = A(v, v, ACT.Identity, bias=modT[:, l, shift * 8 + k, r:r + 1],
                                 scale=alpha[:, j, k, r:r + 1])
                    last.then_inc(S["n_h"], 1)

            act.wait_ge(S["x_banks"], 1)
            A(col[:], ps[7][:, 0:384], ACT.Copy).then_inc(S["cols_ready"], 1)
            act.wait_ge(S["cols_ready"], 1)
            A(csT[:, :, 0], vc(V_CC, 8), ACT.Silu)
            A(csT[:, :, 1], vc(V_C, 8), ACT.Silu).then_inc(S["silu_c"], 1)
            act.wait_ge(S["misc_in"], 16 * 6)
            act.wait_ge(S["dcol_op"], 1)
            act.wait_ge(S["x_banks"], 9)
            norm_act(0, 0, 0, 0)
            act.wait_ge(S["dt_v"], 1)
            A(dts[1][0:64, :], dts[0][0:64, :], ACT.Abs).then_inc(S["dt_act"], 1)
            act.wait_ge(S["dt_act"], 1)
            A(dts[1][0:64, :], dts[1][0:64, :], ACT.Exp, scale=-1.0).then_inc(S["dt_act"], 1)
            A(nega, nega, ACT.Exp).then_inc(S["dt_act"], 1)
            act.wait_ge(S["dt_v"], 2)
            A(dts[3][0:64, :], dts[2][0:64, :], ACT.Ln).then_inc(S["dt_act"], 1)

            def evac_raw(g, t):
                act.wait_ge(S["gemm_done"], 6 * g + t + 1)
                A(raw[:, t, :, 2:2 + 256], ps[t % 2][:].rearrange("p (s t) -> p s t", s=2), ACT.Copy)\
                    .then_inc(S["gemm_evac"], 1)

            def evac_z(g, t):
                act.wait_ge(S["gemm_done"], 6 * g + 5 + t)
                A(zs[:, t, :], ps[t][:], ACT.Silu).then_inc(S["gemm_evac"], 1)

            act.wait_ge(S["dcol_op"], 2)
            evac_raw(0, 0)
            evac_raw(0, 1)
            act.wait_ge(S["dt_tr"], 1)
            A(dtk, ps[3][:, 0:256], ACT.Copy)
            A(atk, ps[3][:, 256:512], ACT.Copy).then_inc(S["dt_tok"], 1)
            evac_raw(0, 2)
            evac_raw(0, 3)
            act.wait_ge(S["ac_ps"], 1)
            for d in range(2):
                last = A(acum[:, :, 32 * d:32 * d + 32], ps[4][:, 128 * d:128 * d + 128].rearrange("p (c h) -> p c h", c=NCH), ACT.Copy)
            last.then_inc(S["ac_sb"], 1)
            A(dec, ps[4][:, 256:512].rearrange("p (c h) -> p c h", c=NCH), ACT.Exp).then_inc(S["ac_exp"], 1)
            evac_z(0, 0)
            evac_z(0, 1)
            act.wait_ge(S["ac_tail"], 1)
            A(tail, tail, ACT.Exp).then_inc(S["ac_exp"], 1)
            act.wait_ge(S["ac_rows"], 1)
            A(dts[2][0:64, :], ps[2][0:64, :], ACT.Copy).then_inc(S["ac_rows_sb"], 1)
            act.wait_ge(S["ac_rows_sb"], 1)
            act.dma_start(scr, dts[2][0:64, :]).then_inc(S["scr_out"], 16)
            act.wait_ge(S["scr_out"], 16)

            def conv_silu(g):
                for t in range(4):
                    act.wait_ge(S["conv_step"], 20 * g + 17 + t)
                    A(cx[:, t, :], cx[:, t, :], ACT.Silu,
                      bias=vc(V_CB + (2 * g + t if t < 2 else 16 + 8 * (t - 2) + g))).then_inc(S["cx_ready"], 1)

            def step(g, first=False, more=True):
                if more:
                    evac_raw(g + 1, 0)
                    evac_raw(g + 1, 1)
                if not first:
                    act.wait_ge(S["gsum_done"], g)
                    A(grs, ps[5][:], ACT.Sqrt, bias=eps, scale=1.0 / 256).then_inc(S["grs_done"], 1)
                for n in range(4):
                    act.wait_ge(S["tr_ready"], 4 * g + n + 1)
                    dst = (xtok[:, 0:2, :], xtok[:, 2:4, :], btok, cbT)[n]
                    A(dst, ps[2 + n][:], ACT.Copy).then_inc(S["tok_evac"], 1)
                for d in range(2):
                    act.wait_ge(S["seg_op"], 2 * g + d + 1)
                    A(rowb[d], rowb[d], ACT.Exp).then_inc(S["er_done"], 1)
                for d in range(2):
                    act.wait_ge(S["seg_mask"], 2 * g + d + 1)
                    A(seg[d], seg[d], ACT.Exp).then_inc(S["e_done"], 1)
                if more:
                    evac_raw(g + 1, 2)
                    evac_raw(g + 1, 3)
                    conv_silu(g + 1)
                for t in range(2):
                    act.wait_ge(S["yg_done"], 2 * g + t + 1)
                    A(ysq[:, t, :], yb[:, t, :], ACT.Square).then_inc(S["ysq_done"], 1)
                if more:
                    evac_z(g + 1, 0)
                    evac_z(g + 1, 1)

            conv_silu(0)
            step(0, first=True)
            with act.Fori(1, 7) as g:
                step(g)
            step(7, more=False)
            act.wait_ge(S["gsum_done"], 8)
            A(grs, ps[5][:], ACT.Sqrt, bias=eps, scale=1.0 / 256).then_inc(S["grs_done"], 1)
            norm_act(1, 0, 0, 3)

            with act.Fori(0, FF_BLOCKS) as b:
                for q in range(2):
                    act.wait_ge(S["ff_done"], 4 * b + 2 * q + 1)
                    act.wait_ge(S["ff_pair_free"], 2 * b + q + 1)
                    A(sil[q], ps[2 * q][:], ACT.Silu).then_inc(S["ff_sil"], 1)
            norm_act(2, 1, 0, 0)

            for n in range(10):
                act.wait_ge(S["q_ps"], n + 1)
                is_k = n in (4, 5)
                if is_k:
                    A(kTt[:, n - 4, :], ps[n % 2][:], ACT.Identity, bias=vc(V_BK + n - 4)).then_inc(S["q_pre"], 1)
                else:
                    t = n if n < 4 else n - 2
                    A(qT[:, t, :], ps[n % 2][:, 0:256], ACT.Identity, bias=vc(V_BQ + t)).then_inc(S["q_pre"], 1)

            def head_of(u):
                t, a = u // 4, (u // 2) % 2
                return 8 * (t // 4) + 4 * a + t % 4

            def exp_unit(u):
                act.wait_ge(S["s_nm"], u + 1)
                o = 8 * (u % 3)
                A(stat[:, o + 3:o + 4], sinkc[:, head_of(u):head_of(u) + 1], ACT.Exp, bias=stat[:, o + 1:o + 2])
                A(sc[u % 3], sc[u % 3], ACT.Exp, bias=stat[:, o + 1:o + 2], accum_out=stat[:, o + 2:o + 3])\
                    .then_inc(S["s_exp"], 1)

            def copy_pt(u):
                act.wait_ge(S["s_pt"], u + 1)
                if u >= 2:
                    act.wait_ge(S["s_pv"], u - 1)
                A(pT[u % 2], ps[2 + u % 2][:], ACT.Copy).then_inc(S["s_ptc"], 1)

            for u in range(34):
                if u < 32:
                    exp_unit(u)
                if u >= 2:
                    copy_pt(u - 2)
            norm_act(3, 1, 0, 3, lat=True)
            act.wait_ge(S["rt_op"], 6)
            for tt in range(2):
                last = A(gts[:, tt:tt + 1], gts[:, tt:tt + 1], ACT.Exp)
            last.then_inc(S["rt_act"], 1)
            for n in range(4):
                act.wait_ge(S["h2_ps"], n + 1)
                tt, hf = n // 2, n % 2
                A(h2k[:, tt, hf * 512:hf * 512 + 512], ps[2 + n][:], ACT.Copy).then_inc(S["h2_sb"], 1)

            def x_high(E, par):
                act.wait_ge(S["ga_ps"], E + 1)
                for j in range(2):
                    A(x_hi[:, par, 4 * j:4 * j + 4, :], ps[4 + j][:], ACT.Copy).then_inc(S["xhi_done"], 1)

            def experts(ps_):
                with act.Fori(0, 4) as pr:
                    NP = pr + 4 * ps_
                    for h in range(2):
                        E = 2 * NP + h

                        def used(load):
                            return UNITS + E_UNITS * h + 2 * E_AT[load] + 2

                        def high(kind, b):
                            for half in range(2 if kind == "up" else 1):
                                n = E_LOADS * h + E_AT[(kind, b, half)]
                                s = n % STAGES
                                act.wait_ge(stage_in[s], 32 * (2 * E_LOADS // STAGES * NP + n // STAGES + 1))
                                for q in range(2):
                                    at = 2 * n + q
                                    act.wait_ge(S["w_used"], 2 * E_UNITS * NP + at + 1)
                                    A(w_hi[:, at % UNITS, :], stages[s][:, q * 1024:q * 1024 + 1024], ACT.Copy)\
                                        .then_inc(S["whi_done"], 1)

                        high("up", 0)
                        high("up", 1)
                        for b in range(E_BLOCKS):
                            act.wait_ge(S["w_used"], 2 * E_UNITS * NP + used(("up", b, 1)))
                            A(msil[b % 2], ps[b % 2][:, 0:256], ACT.Silu).then_inc(S["msil_done"], 1)
                            if b == 2:
                                act.wait_ge(S["gx_ps"], E + 1)
                                A(Pg, ps[4][:, 0:256], ACT.Copy).then_inc(S["pg_done"], 1)
                            if b + 2 < E_BLOCKS:
                                high("up", b + 2)
                            act.wait_ge(S["mt_ps"], E_BLOCKS * E + b + 1)
                            A(h_hi[:, b % 2, :], ps[6 + b % 2][:, 0:256], ACT.Copy).then_inc(S["hhi_done"], 1)
                            if b + 1 < E_BLOCKS:
                                high("down", b)
                            if b == E_BLOCKS - 2:
                                high("down", b + 1)
                            if b == 8:
                                x_high(E + 1, 1 - h)
                        act.wait_ge(S["w_used"], 2 * E_UNITS * NP + used(("down", E_BLOCKS - 1, 0)))
                        act.wait_ge(S["sc_ps"], 4 * E + 4)
                        for hf in range(2):
                            A(ye[:, hf * 512:hf * 512 + 512], ps[2 + hf][:], ACT.Copy).then_inc(S["ye_done"], 1)

            act.sem_inc(S["ye_done"], 2)
            act.sem_inc(S["w_used"], UNITS)
            act.sem_inc(S["sc_ps"], 4)
            x_high(0, 0)
            experts(0)
            act.wait_ge(S["flag_done"], 1)
            over = act.value_load(flag[0:1, 0:1], min_val=0, max_val=1)
            with act.If(over > 0):
                experts(1)
            norm_act(4, 1, 0, None, lat=True)
            for tt in range(2):
                for hf in range(2):
                    act.wait_ge(S["fin_ps"], 2 * tt + hf + 1)
                    A(otm[:, tt, hf * 512:hf * 512 + 512], ps[2 * tt + hf][:], ACT.Copy).then_inc(S["fin_sb"], 1)

        @block.vector
        def _(dv):
            TS, TT, STT = dv.tensor_scalar, dv.tensor_tensor, dv.scalar_tensor_tensor

            def norm_dve(j, lat=False):
                t0, nt = (256, 256) if lat else (0, 512)
                dv.wait_ge(S["n_rs"], j + 1)
                dv.reciprocal(rs[:, 0:nt], rs[:, 0:nt]).then_inc(S["n_rinv"], 1)
                dv.wait_ge(S["n_rinv"], j + 1)
                for k in range(KT):
                    TT(hT[:, k, t0:t0 + nt], xT[:, k, t0:t0 + nt], rs[:, 0:nt], ALU.mult).then_inc(S["n_mul"], 1)

            def alphas(j, l, scale, wrow):
                STT(alpha[:, j], modT[:, l, scale * 8:scale * 8 + 8, :], 1.0,
                    vc(wrow, 8).unsqueeze(2).to_broadcast([P, 8, 2]), ALU.add, ALU.mult).then_inc(S["alpha_done"], 1)

            def mod_rows(n, banks, w, at=0):
                dv.wait_ge(S["moda_ps"], n + 1)
                for j, bank in enumerate(banks):
                    last = dv.tensor_copy(mrow[:, at + j * w:at + j * w + w], ps[bank][0:2, 0:w])
                last.then_inc(S["mrow_sb"], 1)

            def mod_out(l, t0, nt, n, bank):
                dv.wait_ge(S["modt_ps"], n + 1)
                dst = modT[:, l, t0:t0 + nt, :] if isinstance(t0, int) else modT[:, l, bass.ds(t0, nt), :]
                TT(dst, ps[bank][:, 0:2 * nt].rearrange("p (m r) -> p m r", m=nt),
                   vc(V_BMOD + 48 * l + t0, nt).unsqueeze(2).to_broadcast([P, nt, 2]), ALU.add).then_inc(S["mod_done"], 1)

            dv.sem_inc(S["wlo_done"], 2 * STAGES)
            dv.memset(eps, EPS)
            dv.memset(one, 1.0).then_inc(S["dcol_op"], 1)
            for k in range(KT):
                dv.wait_ge(S["x_banks"], k + 2)
                if k == 7:
                    dv.wait_ge(S["cols_ready"], 1)
                dv.tensor_copy(xT[:, k, :], ps[k][:]).then_inc(S["xres"], 1)
            dv.wait_ge(S["misc_in"], 16 * 6)
            for j in range(5):
                if j < 4:
                    mod_rows(j, (5 + j % 2,), 512, 512 * (j % 2))
                if j:
                    mod_out(0, 4 * (j - 1), 4, j - 1, 3 + (j - 1) % 2)
            dv.wait_ge(S["mod_done"], 4)
            alphas(0, 0, 1, V_N1)
            norm_dve(0)
            dv.memset(raw[:, :, :, 0:2], 0.0)
            dv.memset(raw[:, :, :, 258:260], 0.0).then_inc(S["dcol_op"], 1)
            for q in range(2):
                r = slice(64 * q, 64 * q + 64)
                last = TT(dcol[r, :], dbc[r, q:32:2], dbc[r, 32 + q:64:2], ALU.add)
            last.then_inc(S["dcol_op"], 1)
            v, e, w, lw, dt_, a_ = (t[0:64, :] for t in dts)
            dv.wait_ge(S["dt_ps"], 1)
            TS(v, ps[2][0:64, :], dtb, None, ALU.add).then_inc(S["dt_v"], 1)
            dv.wait_ge(S["dt_act"], 3)
            TS(w, e, 1.0, None, ALU.add).then_inc(S["dt_v"], 1)
            dv.wait_ge(S["dt_v"], 2)
            dv.wait_ge(S["dt_act"], 4)
            n = 2

            def link(ins):
                nonlocal n
                n += 1
                ins.then_inc(S["dt_v"], 1)
                dv.wait_ge(S["dt_v"], n)

            link(TS(w, w, -1.0, None, ALU.add))
            link(TS(a_, w, 0.0, None, ALU.is_equal))
            link(TT(w, w, a_, ALU.add))
            link(TT(a_, a_, e, ALU.mult))
            link(dv.reciprocal(w, w))
            link(TT(lw, lw, w, ALU.mult))
            link(TT(lw, lw, e, ALU.mult))
            link(TT(lw, lw, a_, ALU.add))
            link(STT(dt_, v, 0.0, lw, ALU.max, ALU.add))
            TS(a_, dt_, nega, -1.0, ALU.mult, ALU.mult).then_inc(S["dt_dve"], 1)
            dv.wait_ge(S["ac_sb"], 1)
            dv.wait_ge(S["ac_exp"], 1)
            TT(tail, ps[4][:, 256:512].rearrange("p (c h) -> p c h", c=NCH), acum, ALU.subtract).then_inc(S["ac_tail"], 1)
            dv.wait_ge(S["ac_exp"], 2)
            TT(tail, tail, dtk, ALU.mult).then_inc(S["ac_tail"], 1)
            dv.wait_ge(S["ac_tail"], 2)

            def conv_row(g, t):
                return 2 * g + t if t < 2 else 16 + 8 * (t - 2) + g

            def finish(g):
                dv.wait_ge(S["grs_done"], g)
                dv.reciprocal(grs, grs).then_inc(S["grinv_done"], 1)
                dv.wait_ge(S["grinv_done"], g)
                for t in range(2):
                    r = 2 * (g - 1) + t
                    dst = gT[:, r, :] if isinstance(r, int) else gT[:, bass.ds(r, 1), :].rearrange("p a t -> p (a t)")
                    STT(dst, yb[:, t, :], vc(V_SN + r), grs, ALU.mult, ALU.mult).then_inc(S["gT_done"], 1)

            def per_token(v, d, g):
                a = v[:, :, bass.ds(32 * d + 4 * g, 4)] if not isinstance(g, int) else v[:, :, 32 * d + 4 * g:32 * d + 4 * g + 4]
                return a

            def convolve(g, first=False):
                for k in range(CONV_K):
                    for t in range(4):
                        if k == 0:
                            dv.wait_ge(S["gemm_evac"], 6 * g + t + 1)
                            if t == 0 and not first:
                                dv.wait_ge(S["sk_done"], 2 * g)
                                dv.wait_ge(S["ce_done"], 2 * g)
                        else:
                            dv.wait_ge(S["conv_step"], 20 * g + 4 * (k - 1) + t + 1)
                        src = raw[:, t, :, k:k + 256]
                        dst = cx[:, t, :].rearrange("p (s t) -> p s t", s=2)
                        wk = vc(V_CW + 32 * k + conv_row(g, t))
                        if k == 0:
                            ins = TS(dst, src, wk, None, ALU.mult)
                        else:
                            ins = STT(dst, src, wk, dst, ALU.mult, ALU.add)
                        ins.then_inc(S["conv_step"], 1)

            def step(g, first=False, more=True):
                dv.wait_ge(S["rowb_in"], 32 * g + 32)
                for d in range(2):
                    o = seg[d].rearrange("p h (c i) -> p h c i", c=NCH)
                    i0 = rowb[d].rearrange("p h (c i) -> p h c i", c=NCH)
                    for ch in range(NCH):
                        a = per_token(acum, d, g)[:, ch, :].unsqueeze(2).to_broadcast([P, HPG, P])
                        last = TT(o[:, :, ch, :], i0[:, :, ch, :], a, ALU.subtract)
                    last.then_inc(S["seg_op"], 1)
                if not first:
                    mod_out(0, 12 + 4 * g, 4, 3 + g, 5)
                    finish(g)
                dv.wait_ge(S["tok_evac"], 4 * g + 2)
                if not first:
                    dv.wait_ge(S["gT_done"], 2 * g)
                for f, dst in ((tail, xtl), (dtk, xdt)):
                    for d in range(2):
                        a = per_token(f, d, g).unsqueeze(3).to_broadcast([P, NCH, HPG, HD])
                        TT(dst[d].rearrange("p c (h q) -> p c h q", h=HPG), xtok.rearrange("p c (h q) -> p c h q", h=HPG),
                           a, ALU.mult).then_inc(S["xs_ready"], 1)
                for d in range(2):
                    dv.wait_ge(S["er_done"], 2 * g + d + 1)
                    TT(rowb[d], rowb[d], cx[:, 3, :].unsqueeze(1).to_broadcast([P, HPG, NTOK]), ALU.mult)\
                        .then_inc(S["ce_done"], 1)
                dv.wait_ge(S["tok_evac"], 4 * g + 4)
                for d in range(2):
                    dv.wait_ge(S["e_done"], 2 * g + d + 1)
                    TT(seg[d], seg[d], cbT.unsqueeze(1).to_broadcast([P, HPG, NTOK]), ALU.mult).then_inc(S["m_done"], 1)
                dv.wait_ge(S["st_ready"], g + 1)
                adds = {(0, 0): ps[2][:, 0:256], (0, 1): ps[2][:, 256:512], (0, 2): ps[3][:, 0:256],
                        (1, 1): ps[3][:, 256:512], (1, 0): ps[4][:, 0:256], (1, 3): ps[4][:, 256:512]}
                n = 10 * g
                dv.tensor_copy(stt_[:, 0, :], adds[(0, 0)]).then_inc(S["st_op"], 1)
                dv.tensor_copy(stt_[:, 3, :], adds[(1, 1)]).then_inc(S["st_op"], 1)
                n = n + 2
                for lvl in range(2):
                    pair = (((0, 1 + lvl), lvl, 1 + lvl), ((1, (0, 3)[lvl]), 3 + lvl, 4 + lvl))
                    for (d, ch), s0, s1 in pair:
                        dv.wait_ge(S["st_op"], n)
                        a = per_token(dec, d, g)[:, ch, :].unsqueeze(2).to_broadcast([P, HPG, HD])
                        TT(stt_[:, s1, :].rearrange("p (h q) -> p h q", h=HPG),
                           stt_[:, s0, :].rearrange("p (h q) -> p h q", h=HPG), a, ALU.mult).then_inc(S["st_op"], 1)
                    n = n + 2
                    for (d, ch), s0, s1 in pair:
                        dv.wait_ge(S["st_op"], n)
                        TT(stt_[:, s1, :], stt_[:, s1, :], adds[(d, ch)], ALU.add).then_inc(S["st_op"], 1)
                    n = n + 2
                for t in range(2):
                    dc = dcol[:, 2 * g + t:2 * g + t + 1] if isinstance(g, int) else dcol[:, bass.ds(2 * g + t, 1)]
                    TS(yb[:, t, :], cx[:, t, :], dc, None, ALU.mult).then_inc(S["sk_done"], 1)
                if more:
                    convolve(g + 1)
                mod_rows(4 + g, (5,), 512)
                dv.wait_ge(S["sk_done"], 2 * g + 2)
                for t in range(2):
                    dv.wait_ge(S["y_ready"], 2 * g + t + 1)
                    TT(yb[:, t, :], yb[:, t, :], ps[6 + t][:], ALU.add).then_inc(S["ys_done"], 1)
                for t in range(2):
                    dv.wait_ge(S["ys_done"], 2 * g + t + 1)
                    dv.wait_ge(S["gemm_evac"], 6 * g + 5 + t)
                    TT(yb[:, t, :], yb[:, t, :], zs[:, t, :], ALU.mult).then_inc(S["yg_done"], 1)

            dv.wait_ge(S["dcol_op"], 3)
            convolve(0, first=True)
            step(0, first=True)
            with dv.Fori(1, 7) as g:
                step(g)
            step(7, more=False)
            mod_out(0, 44, 4, 11, 5)
            finish(8)
            dv.wait_ge(S["mod_done"], 12)
            alphas(1, 0, 4, V_N2)

            def residual(k, bank, l, gate):
                for r in range(2):
                    v = xT[:, k, r * 256:r * 256 + 256]
                    last = STT(v, ps[bank][:, r * 256:r * 256 + 256], modT[:, l, gate * 8 + k, r:r + 1], v,
                               ALU.mult, ALU.add)
                last.then_inc(S["xres"], 1)

            for k in range(KT):
                dv.wait_ge(S["wo_done"], k + 1)
                residual(k, k % 2, 0, 2)
            dv.sem_inc(S["ff_pair_free"], 2)
            norm_dve(1)

            def ff_mul(b):
                for q in range(2):
                    dv.wait_ge(S["ff_sil"], 2 * b + q + 1)
                    dv.wait_ge(S["ff_done"], 4 * b + 2 * q + 2)
                    r = 2 * b + q
                    dst = hid[:, r, :] if isinstance(r, int) else hid[:, bass.ds(r, 1), :].rearrange("p a t -> p (a t)")
                    TT(dst, sil[q], ps[2 * q + 1][:], ALU.mult).then_inc(S["ff_pair_free"], 1)

            with dv.Fori(0, 8) as b:
                ff_mul(b)
                mod_rows(12 + b, (5, 6), 384)
                mod_out(1, 6 * b, 6, 12 + b, 4)
            for b in range(8, FF_BLOCKS):
                ff_mul(b)
            dv.wait_ge(S["mod_done"], 20)
            alphas(2, 1, 1, V_N1 + 8)
            alphas(3, 1, 4, V_N2 + 8)
            for k in range(KT):
                dv.wait_ge(S["w2_done"], k + 1)
                residual(k, 4 + k % 2, 0, 5)
            norm_dve(2)

            for n in range(10):
                is_k = n in (4, 5)
                t = n - 4 if is_k else (n if n < 4 else n - 2)
                v = kTt[:, t, 256:512] if is_k else qT[:, t, :]
                dv.wait_ge(S["q_rot"], n + 1)
                if n >= 2:
                    dv.wait_ge(S["q_out"], n - 1)
                TT(rt[n % 2], ps[2 + n % 2][:, 0:256], sinb, ALU.mult).then_inc(S["q_t1"], 1)
                TT(v, v, cosb, ALU.mult).then_inc(S["qkv_free"], 1)
                dv.wait_ge(S["qkv_free"], n + 1)
                TT(v, v, rt[n % 2], ALU.add).then_inc(S["q_out"], 1)
            dv.wait_ge(S["misc_in"], 16 * 7)
            for kt in range(4):
                dv.wait_ge(S["v_ps"], kt + 1)
                if kt % 2:
                    TT(vtk[:, kt, :], ps[4 + kt // 2][:, 256:512], vb, ALU.add).then_inc(S["v_out"], 1)
                else:
                    dv.wait_ge(S["v_ps"], kt + 2)
                    TT(vtk[:, kt, :], ps[4 + kt // 2][:, 0:256], vb, ALU.add).then_inc(S["v_out"], 1)

            dv.wait_ge(S["band_in"], 32)

            def head_of(u):
                t, a = u // 4, (u // 2) % 2
                return 8 * (t // 4) + 4 * a + t % 4

            def soft_a(u):
                o = 8 * (u % 3)
                dv.wait_ge(S["s_ps"], u + 1)
                if u >= 3:
                    dv.wait_ge(S["s_pt"], u - 2)
                b0 = C_BAND + 512 * (u % 2)
                STT(sc[u % 3], ps[(0, 1, 6)[u % 3]][:], 0.125, cst[:, b0:b0 + 512], ALU.mult, ALU.add).then_inc(S["s_sm"], 1)
                dv.wait_ge(S["s_sm"], u + 1)
                dv.reduce_max(stat[:, o:o + 1], sc[u % 3], AX.X).then_inc(S["s_mx"], 1)
                dv.wait_ge(S["s_mx"], u + 1)
                TS(stat[:, o + 1:o + 2], stat[:, o:o + 1], sinkc[:, head_of(u):head_of(u) + 1], -1.0,
                   ALU.max, ALU.mult).then_inc(S["s_nm"], 1)

            def soft_b(u):
                o = 8 * (u % 3)
                dv.wait_ge(S["s_exp"], u + 1)
                TT(stat[:, o + 4:o + 5], stat[:, o + 2:o + 3], stat[:, o + 3:o + 4], ALU.add).then_inc(S["s_den"], 1)
                dv.wait_ge(S["s_den"], u + 1)
                dv.reciprocal(stat[:, o + 5:o + 6], stat[:, o + 4:o + 5]).then_inc(S["s_rd"], 1)
                dv.wait_ge(S["s_rd"], u + 1)
                TS(sc[u % 3], sc[u % 3], stat[:, o + 5:o + 6], None, ALU.mult).then_inc(S["s_p"], 1)

            for u in range(33):
                if u < 32:
                    soft_a(u)
                if u >= 1:
                    soft_b(u - 1)
                    if u % 4 == 3 and u > 4:
                        t = u // 4 - 1
                        dv.wait_ge(S["s_pv"], 4 * t + 4)
                        dv.tensor_copy(oT[:, t, :], ps[4 + t % 2][:, 0:256]).then_inc(S["o_out"], 1)
            dv.wait_ge(S["s_pv"], 32)
            dv.tensor_copy(oT[:, 7, :], ps[5][:, 0:256]).then_inc(S["o_out"], 1)
            for k in range(KT):
                dv.wait_ge(S["wo_done"], 8 + k + 1)
                if k >= 2:
                    dv.wait_ge(S["xres"], 24 + k - 1)
                TS(rt[k % 2], ps[k % 2][:, 0:256], vc(V_BO + k), modT[:, 1, 16 + k, 1:2], ALU.add, ALU.mult)\
                    .then_inc(S["at_y"], 1)
                dv.wait_ge(S["at_y"], k + 1)
                v = xT[:, k, 256:512]
                TT(v, v, rt[k % 2], ALU.add).then_inc(S["xres"], 1)
            norm_dve(3, lat=True)

            dv.wait_ge(S["lg_ps"], 1)
            r = 0

            def rlink(ins):
                nonlocal r
                r += 1
                ins.then_inc(S["rt_op"], 1)
                dv.wait_ge(S["rt_op"], r)

            rlink(dv.tensor_copy(logit, ps[0][:, 0:16].rearrange("p (a e) -> p a e", a=2)))
            rlink(dv.max(mx8[:, 0, :], logit[:, 0, :]))
            rlink(dv.max(mx8[:, 1, :], logit[:, 1, :]))
            dv.max_index(idx[:, 0, :], mx8[:, 0, :], logit[:, 0, :])
            rlink(dv.max_index(idx[:, 1, :], mx8[:, 1, :], logit[:, 1, :]))
            rlink(dv.tensor_copy(idf, idx))
            rlink(TT(gts[:, 0:2], mx8[:, :, 1], mx8[:, :, 0], ALU.subtract))
            for tt in range(2):
                TS(oh1[:, tt, :], iota8, idf[:, tt, 0:1], None, ALU.is_equal)
            rlink(TS(oh2[:, 0, :], iota8, idf[:, 0, 1:2], None, ALU.is_equal))
            rlink(TS(oh2[:, 1, :], iota8, idf[:, 1, 1:2], None, ALU.is_equal))
            dv.wait_ge(S["rt_act"], 1)
            rlink(TS(gts[:, 2:4], gts[:, 0:2], 1.0, None, ALU.add))
            rlink(dv.reciprocal(gts[:, 4:6], gts[:, 2:4]))
            rlink(TT(gts[:, 6:8], gts[:, 0:2], gts[:, 4:6], ALU.mult))
            rlink(TT(sel, oh1, oh2, ALU.add))
            for tt in range(2):
                TS(oh1[:, tt, :], oh1[:, tt, :], gts[:, 4 + tt:5 + tt], None, ALU.mult)
            rlink(dv.memset(macc, 0.0))
            for tt in range(2):
                rlink(STT(comb[:, tt, 0:8], oh2[:, tt, :], gts[:, 6 + tt:7 + tt], oh1[:, tt, :], ALU.mult, ALU.add))
            dv.wait_ge(S["rk_ps"], 1)
            rlink(STT(pos[:, :, 0:8], ps[1][:, 0:16].rearrange("p (a e) -> p a e", a=2), 1.0, sel, ALU.add, ALU.mult))
            rlink(TS(pos[:, :, 0:8], pos[:, :, 0:8], -1.0, None, ALU.add))
            rlink(TS(pos2[:, :, 0:8], pos[:, :, 0:8], -128.0, None, ALU.add))
            dv.memset(pos2[:, :, 8:9], -1.0)
            dv.tensor_copy(comb[:, :, 8:9], comb[:, :, 0:1])
            rlink(dv.tensor_copy(pos[:, :, 8:9], pos2[:, :, 0:1]))
            rlink(dv.reduce_max(gts[:, 8:9], ps[1][:, 16:24], AX.X))
            rlink(TS(gts[:, 9:10], gts[:, 8:9], 128.0, None, ALU.is_gt))
            dv.tensor_copy(flag[:, 0:1], gts[:, 9:10]).then_inc(S["flag_done"], 1)
            dv.sem_inc(S["macc_op"], 5)
            dv.sem_inc(S["gh_done"], 2)
            dv.sem_inc(S["hlo_done"], 2)

            def masks(E, e, pv):
                at = slice(e, e + 1) if isinstance(e, int) else bass.ds(e, 1)
                for tt in range(2):
                    TS(G[:, tt, :], iota, pv[:, tt, at], None, ALU.is_equal).then_inc(S["g_op"], 1)
                for tt in range(2):
                    TS(Gg[:, tt, :], iota, pv[:, tt, at], comb[:, tt, at], ALU.is_equal, ALU.mult).then_inc(S["g_op"], 1)

            def x_low(E, par):
                for j in range(2):
                    dv.wait_ge(S["xhi_done"], 2 * E + j + 1)
                    TT(x_lo[:, par, 4 * j:4 * j + 4, :], ps[4 + j][:].rearrange("p (k s) -> p k s", k=4),
                       x_hi[:, par, 4 * j:4 * j + 4, :].bitcast(F32), ALU.subtract).then_inc(S["xlo_done"], 1)

            def experts(ps_, pv):
                with dv.Fori(0, 4) as pr:
                    NP = pr + 4 * ps_
                    for h in range(2):
                        e = 2 * pr + h
                        E = 2 * NP + h

                        def low(kind, b):
                            for half in range(2 if kind == "up" else 1):
                                n = E_LOADS * h + E_AT[(kind, b, half)]
                                for q in range(2):
                                    at = 2 * n + q
                                    u = at % UNITS
                                    dv.wait_ge(S["whi_done"], 2 * E_UNITS * NP + at + 1)
                                    TT(w_lo[:, u, :], stages[n % STAGES][:, q * 1024:q * 1024 + 1024],
                                       w_hi[:, u, :].bitcast(F32), ALU.subtract).then_inc(S["wlo_done"], 1)

                        low("up", 0)
                        low("up", 1)
                        for b in range(E_BLOCKS):
                            dv.wait_ge(S["msil_done"], E_BLOCKS * E + b + 1)
                            dv.wait_ge(S["hlo_done"], E_BLOCKS * E + b + 1)
                            TT(gh[b % 2], msil[b % 2], ps[b % 2][:, 256:512], ALU.mult).then_inc(S["gh_done"], 1)
                            if b + 2 < E_BLOCKS:
                                low("up", b + 2)
                            dv.wait_ge(S["hhi_done"], E_BLOCKS * E + b + 1)
                            TT(h_lo[:, b % 2, :], ps[6 + b % 2][:, 0:256], h_hi[:, b % 2, :].bitcast(F32), ALU.subtract)\
                                .then_inc(S["hlo_done"], 1)
                            if b + 1 < E_BLOCKS:
                                low("down", b)
                            if b == E_BLOCKS - 2:
                                low("down", b + 1)
                            if b == 6:
                                dv.wait_ge(S["gx_ps"], E + 1)
                                masks(E + 1, e + 1, pv)
                            if b == 8:
                                x_low(E + 1, 1 - h)
                        for j in range(4):
                            dv.wait_ge(S["sc_ps"], 4 * E + j + 5)
                            v = macc[:, 2 * j:2 * j + 2, :]
                            TT(v, v, ps[4 + j % 2][:].rearrange("p (a t) -> p a t", a=2), ALU.add)\
                                .then_inc(S["macc_op"], 1)

            masks(0, 0, pos)
            x_low(0, 0)
            experts(0, pos)
            dv.wait_ge(S["macc_op"], 5 + 32)
            over = dv.value_load(flag[0:1, 0:1], min_val=0, max_val=1)
            with dv.If(over > 0):
                experts(1, pos2)
                dv.wait_ge(S["macc_op"], 5 + 64)
            for k in range(KT):
                v = xT[:, k, 256:512]
                STT(v, macc[:, k, :], modT[:, 1, 40 + k, 1:2], v, ALU.mult, ALU.add).then_inc(S["xres"], 1)
            dv.wait_ge(S["n_rs"], 5)
            dv.reciprocal(rs[:, 0:256], rs[:, 0:256]).then_inc(S["n_rinv"], 1)
            dv.wait_ge(S["n_rinv"], 5)
            for k in range(KT):
                STT(hT[:, k, 0:256], xT[:, k, 256:512], vc(V_FIN + k), rs[:, 0:256], ALU.mult, ALU.mult)\
                    .then_inc(S["fin_o"], 1)


_INS = ['x', 'c', 'ctx', 'c_ctx', 'w_mod', 'b_mod', 'norm1_w', 'norm2_w', 'ssd_w_in', 'ssd_conv_w', 'ssd_conv_b',
        'ssd_dt_bias', 'ssd_a_log', 'ssd_d', 'ssd_norm_w', 'ssd_w_out', 'attn_w_qkv', 'attn_b_qkv', 'attn_sink',
        'attn_w_o', 'attn_b_o', 'ffn_w1', 'ffn_w3', 'ffn_w2', 'moe_router', 'moe_w1', 'moe_w3', 'moe_w2',
        'final_norm_w']


def kernel(**inputs):
    import numpy as _np
    import concourse.bacc as _bacc
    from concourse import mybir as _mybir
    from concourse.bass_utils import run_bass_kernel_spmd as _run

    nc = _bacc.Bacc("TRN2", target_bir_lowering=False, num_devices=1)
    arrays, args = {}, []
    for name in _INS:
        a = _np.ascontiguousarray(inputs[name])
        arrays[f"in_{name}"] = a
        args.append(nc.dram_tensor(f"in_{name}", a.shape, _mybir.dt.from_np(a.dtype), kind="ExternalInput").ap())
    a = shape_constants()
    arrays["in_consts"] = a
    args.append(nc.dram_tensor("in_consts", a.shape, _mybir.dt.from_np(a.dtype), kind="ExternalInput").ap())
    args.append(nc.dram_tensor("out_0", (1, NLAT, D), F32, kind="ExternalOutput").ap())
    backbone(nc, *args)
    r = _run(nc, [arrays], core_ids=[0])
    return r.results[0]["out_0"]
```
